# Optimizing a Trainium2 kernel written in Bass

```python
import math
import jax, jax.numpy as jnp
from jax import lax
import numpy as np

D_MODEL = 1024
BATCH = 1
SEQ = 512
DEPTH = 1

CHUNK = 64
PLE_DIM = 256
RMS_EPS = 1e-6

DA_HEADS = 8
DA_QK_DIM = 64
DA_V_DIM = 2 * DA_QK_DIM
Q_BLOCK = 128

SSD_EXPAND = 2
SSD_D_INNER = SSD_EXPAND * D_MODEL
SSD_HEAD_DIM = 64
SSD_HEADS = SSD_D_INNER // SSD_HEAD_DIM
SSD_GROUPS = 4
SSD_HEADS_PER_GROUP = SSD_HEADS // SSD_GROUPS
SSD_STATE = 128
SSD_CONV = 4
SSD_CONV_DIM = SSD_D_INNER + 2 * SSD_GROUPS * SSD_STATE

N_EXPERTS = 32
TOP_K = 4
D_EXPERT = D_MODEL
SWIGLU_LIMIT = 7.0
SWIGLU_ALPHA = 1.702

Q_W = DA_HEADS * 2 * DA_QK_DIM
K_W = DA_HEADS * 2 * DA_QK_DIM
V_W = DA_HEADS * DA_V_DIM
Z_W = SSD_D_INNER
XBC_W = SSD_CONV_DIM
DT_W = SSD_HEADS
GATE_W = D_MODEL
IN_W = Q_W + K_W + V_W + Z_W + XBC_W + DT_W + 2 * GATE_W
IN_SPLITS = (
    Q_W,
    Q_W + K_W,
    Q_W + K_W + V_W,
    Q_W + K_W + V_W + Z_W,
    Q_W + K_W + V_W + Z_W + XBC_W,
    Q_W + K_W + V_W + Z_W + XBC_W + DT_W,
    Q_W + K_W + V_W + Z_W + XBC_W + DT_W + GATE_W,
)

kernel_name = "hybrid_diffattn_ssd_moe_streaming_block"

def rms_norm(x, w):
    x32 = x.astype(jnp.float32)
    y = x32 * lax.rsqrt(jnp.mean(x32 * x32, axis=-1, keepdims=True) + RMS_EPS)
    return (y * w.astype(jnp.float32)).astype(x.dtype)

def alibi_slopes(n_heads):
    return jnp.asarray([2.0 ** (-8.0 * (h + 1) / n_heads) for h in range(n_heads)], dtype=jnp.float32)

def diff_attention(q, k, v, lam, head_norm_w, lambda_init):
    b, s = q.shape[0], q.shape[1]
    n_blocks = s // Q_BLOCK
    scale = DA_QK_DIM ** -0.5
    slopes = alibi_slopes(DA_HEADS)
    kpos = jnp.arange(s, dtype=jnp.int32)
    q_blocks = jnp.moveaxis(q.reshape(b, n_blocks, Q_BLOCK, DA_HEADS, 2, DA_QK_DIM), 1, 0)

    def one_block(args):
        q_blk, blk = args
        qpos = blk * Q_BLOCK + jnp.arange(Q_BLOCK, dtype=jnp.int32)
        scores = jnp.einsum('bqhmd,bkhmd->bhmqk', q_blk, k,
                            preferred_element_type=jnp.float32) * scale
        dist = jnp.abs(qpos[:, None] - kpos[None, :]).astype(jnp.float32)
        allowed = (kpos[None, :] // CHUNK) <= (qpos[:, None] // CHUNK)
        bias = jnp.where(allowed[None], -slopes[:, None, None] * dist[None], -jnp.inf)
        probs = jax.nn.softmax(scores + bias[None, :, None], axis=-1)
        attn = probs[:, :, 0] - lam * probs[:, :, 1]
        return jnp.einsum('bhqk,bkhd->bqhd', attn.astype(v.dtype), v)

    out = lax.map(one_block, (q_blocks, jnp.arange(n_blocks, dtype=jnp.int32)))
    out = jnp.moveaxis(out, 0, 1).reshape(b, s, DA_HEADS, DA_V_DIM)
    out = rms_norm(out, head_norm_w) * (1.0 - lambda_init)
    return out.reshape(b, s, DA_HEADS * DA_V_DIM)

def causal_depthwise_conv(u, w, bias):
    c = u.shape[-1]
    out = lax.conv_general_dilated(
        u, w.reshape(SSD_CONV, 1, c).astype(u.dtype),
        window_strides=(1,), padding=((SSD_CONV - 1, 0),),
        dimension_numbers=('NWC', 'WIO', 'NWC'), feature_group_count=c)
    return out + bias

def ssd_chunked_scan(xs, dt, a, bm, cm):
    b, s = xs.shape[0], xs.shape[1]
    nc = s // CHUNK
    def to_chunks(t):
        return t.reshape(b, nc, CHUNK, *t.shape[2:])
    x_c, dt_c, b_c, c_c = to_chunks(xs), to_chunks(dt), to_chunks(bm), to_chunks(cm)
    acum = jnp.cumsum(dt_c * a, axis=2)
    xdt = x_c * dt_c[..., None]

    idx = jnp.arange(CHUNK)
    causal = (idx[:, None] >= idx[None, :])[:, :, None, None]
    seg = acum[:, :, :, None] - acum[:, :, None, :]
    decay = jnp.exp(jnp.where(causal, seg, -jnp.inf))
    cb = jnp.einsum('bclgn,bcsgn->bclsg', c_c, b_c)
    y_diag = jnp.einsum('bclsgr,bcsgrp->bclgrp', cb[..., None] * decay, xdt)

    decay_to_end = jnp.exp(acum[:, :, -1:] - acum)
    decay_from_start = jnp.exp(acum)
    chunk_decay = jnp.exp(acum[:, :, -1])

    def step(state, inp):
        c_k, b_k, xdt_k, dte_k, dfs_k, cd_k = inp
        y_off = jnp.einsum('blgn,bgrpn,blgr->blgrp', c_k, state, dfs_k)
        new_state = state * cd_k[..., None, None] + jnp.einsum('blgn,blgr,blgrp->bgrpn', b_k, dte_k, xdt_k)
        return new_state, y_off

    state0 = jnp.zeros((b, SSD_GROUPS, SSD_HEADS_PER_GROUP, SSD_HEAD_DIM, SSD_STATE), jnp.float32)
    xs_scan = tuple(jnp.moveaxis(t, 1, 0) for t in (c_c, b_c, xdt, decay_to_end, decay_from_start, chunk_decay))
    _, y_off = lax.scan(step, state0, xs_scan)
    y = y_diag + jnp.moveaxis(y_off, 0, 1)
    return y.reshape(b, s, SSD_GROUPS, SSD_HEADS_PER_GROUP, SSD_HEAD_DIM)

def ssd_mixer(z, xbc, dt_raw, conv_w, conv_b, dt_bias, a_log, d_skip, norm_w):
    f32 = jnp.float32
    b, s = z.shape[0], z.shape[1]
    xbc = jax.nn.silu(causal_depthwise_conv(xbc, conv_w, conv_b))
    xs, bm, cm = jnp.split(xbc, [SSD_D_INNER, SSD_D_INNER + SSD_GROUPS * SSD_STATE], axis=-1)
    xs = xs.reshape(b, s, SSD_GROUPS, SSD_HEADS_PER_GROUP, SSD_HEAD_DIM).astype(f32)
    bm = bm.reshape(b, s, SSD_GROUPS, SSD_STATE).astype(f32)
    cm = cm.reshape(b, s, SSD_GROUPS, SSD_STATE).astype(f32)
    dt = jax.nn.softplus(dt_raw.astype(f32) + dt_bias.astype(f32)).reshape(b, s, SSD_GROUPS, SSD_HEADS_PER_GROUP)
    a = -jnp.exp(a_log.astype(f32)).reshape(SSD_GROUPS, SSD_HEADS_PER_GROUP)
    y = ssd_chunked_scan(xs, dt, a, bm, cm)
    y = y + d_skip.astype(f32).reshape(SSD_GROUPS, SSD_HEADS_PER_GROUP)[:, :, None] * xs
    y = y.reshape(b, s, SSD_D_INNER).astype(z.dtype) * jax.nn.silu(z)
    gsz = SSD_D_INNER // SSD_GROUPS
    y = rms_norm(y.reshape(b, s, SSD_GROUPS, gsz), norm_w.reshape(SSD_GROUPS, gsz))
    return y.reshape(b, s, SSD_D_INNER)

def moe_ffn(h, router_w, router_b, w_up, b_up, w_down, b_down):
    b, s, d = h.shape
    tok = h.reshape(-1, d)
    n_tok = tok.shape[0]
    logits = (tok @ router_w + router_b).astype(jnp.float32)
    top_vals, top_idx = lax.top_k(logits, TOP_K)
    gate_w = jax.nn.softmax(top_vals, axis=-1)
    flat_e = top_idx.reshape(-1)
    order = jnp.argsort(flat_e)
    token_of = order // TOP_K
    e_sorted = flat_e[order]
    group_sizes = jnp.bincount(flat_e, length=N_EXPERTS).astype(jnp.int32)
    x_sorted = tok[token_of]
    gu = lax.ragged_dot(x_sorted, w_up, group_sizes) + b_up[e_sorted]
    g, u = gu[:, :D_EXPERT], gu[:, D_EXPERT:]
    g = jnp.minimum(g, SWIGLU_LIMIT)
    u = jnp.clip(u, -SWIGLU_LIMIT, SWIGLU_LIMIT)
    act = (u + 1.0) * (g * jax.nn.sigmoid(SWIGLU_ALPHA * g))
    out = lax.ragged_dot(act, w_down, group_sizes) + b_down[e_sorted]
    out = out * gate_w.reshape(-1)[order][:, None].astype(out.dtype)
    y = jax.ops.segment_sum(out, token_of, num_segments=n_tok)
    return y.reshape(b, s, d)

def setup_inputs(seed: int = 0) -> dict:
    key = jax.random.key(seed)
    ks = jax.random.split(key, 32)
    f32 = jnp.float32
    L, D = DEPTH, D_MODEL

    def nrm(k, shape, scale):
        return jax.random.normal(k, shape, f32) * scale

    dt_init = jnp.exp(jax.random.uniform(ks[12], (L, SSD_HEADS), f32, math.log(1e-3), math.log(1e-1)))
    return {
        "x": nrm(ks[0], (BATCH, SEQ, D), 1.0),
        "p": nrm(ks[1], (DEPTH, BATCH, SEQ, PLE_DIM), 1.0),
        "mix_norm_w": 1.0 + nrm(ks[2], (L, D), 0.02),
        "w_in": nrm(ks[3], (L, D, IN_W), D ** -0.5),
        "lambda_q1": nrm(ks[4], (L, DA_QK_DIM), 0.1),
        "lambda_k1": nrm(ks[5], (L, DA_QK_DIM), 0.1),
        "lambda_q2": nrm(ks[6], (L, DA_QK_DIM), 0.1),
        "lambda_k2": nrm(ks[7], (L, DA_QK_DIM), 0.1),
        "da_head_norm_w": 1.0 + nrm(ks[8], (L, DA_V_DIM), 0.02),
        "w_attn_branch": nrm(ks[9], (L, V_W, D), V_W ** -0.5),
        "conv_w": nrm(ks[10], (L, SSD_CONV, SSD_CONV_DIM), SSD_CONV ** -0.5),
        "conv_b": nrm(ks[11], (L, SSD_CONV_DIM), 0.02),
        "dt_bias": dt_init + jnp.log(-jnp.expm1(-dt_init)),
        "a_log": jnp.log(jax.random.uniform(ks[13], (L, SSD_HEADS), f32, 1.0, 16.0)),
        "d_skip": 1.0 + nrm(ks[14], (L, SSD_HEADS), 0.02),
        "ssd_norm_w": 1.0 + nrm(ks[15], (L, SSD_D_INNER), 0.02),
        "w_ssd_branch": nrm(ks[16], (L, SSD_D_INNER, D), SSD_D_INNER ** -0.5),
        "w_out": nrm(ks[17], (L, D, D), D ** -0.5),
        "moe_norm_w": 1.0 + nrm(ks[18], (L, D), 0.02),
        "router_w": nrm(ks[19], (L, D, N_EXPERTS), D ** -0.5),
        "router_b": nrm(ks[20], (L, N_EXPERTS), 0.01),
        "w_up": nrm(ks[21], (L, N_EXPERTS, D, 2 * D_EXPERT), D ** -0.5),
        "b_up": nrm(ks[22], (L, N_EXPERTS, 2 * D_EXPERT), 0.01),
        "w_down": nrm(ks[23], (L, N_EXPERTS, D_EXPERT, D), D_EXPERT ** -0.5),
        "b_down": nrm(ks[24], (L, N_EXPERTS, D), 0.01),
        "ple_norm_w": 1.0 + nrm(ks[25], (L, D), 0.02),
        "w_ple_gate": nrm(ks[26], (L, D, D), D ** -0.5),
        "w_ple_proj": nrm(ks[27], (L, PLE_DIM, D), PLE_DIM ** -0.5),
        "final_norm_w": 1.0 + nrm(ks[28], (D,), 0.02),
    }

def reference(x, p, mix_norm_w, w_in, lambda_q1, lambda_k1, lambda_q2, lambda_k2,
              da_head_norm_w, w_attn_branch, conv_w, conv_b, dt_bias, a_log, d_skip,
              ssd_norm_w, w_ssd_branch, w_out, moe_norm_w, router_w, router_b,
              w_up, b_up, w_down, b_down, ple_norm_w, w_ple_gate, w_ple_proj, final_norm_w):
    b, s, _ = x.shape
    f32 = jnp.float32
    for i in range(DEPTH):
        h = rms_norm(x, mix_norm_w[i])
        proj = h @ w_in[i]
        q, k, v, z, xbc, dt_raw, gate_a, gate_s = jnp.split(proj, IN_SPLITS, axis=-1)

        q = q.reshape(b, s, DA_HEADS, 2, DA_QK_DIM)
        k = k.reshape(b, s, DA_HEADS, 2, DA_QK_DIM)
        v = v.reshape(b, s, DA_HEADS, DA_V_DIM)
        lambda_init = 0.8 - 0.6 * math.exp(-0.3 * i)
        lam = (jnp.exp(jnp.sum(lambda_q1[i].astype(f32) * lambda_k1[i].astype(f32)))
               - jnp.exp(jnp.sum(lambda_q2[i].astype(f32) * lambda_k2[i].astype(f32)))
               + lambda_init)
        y_attn = diff_attention(q, k, v, lam, da_head_norm_w[i], lambda_init)

        y_ssd = ssd_mixer(z, xbc, dt_raw, conv_w[i], conv_b[i], dt_bias[i], a_log[i],
                          d_skip[i], ssd_norm_w[i])

        merged = (jax.nn.sigmoid(gate_a) * (y_attn @ w_attn_branch[i])
                  + jax.nn.sigmoid(gate_s) * (y_ssd @ w_ssd_branch[i]))
        x = x + merged @ w_out[i]

        x = x + moe_ffn(rms_norm(x, moe_norm_w[i]), router_w[i], router_b[i],
                        w_up[i], b_up[i], w_down[i], b_down[i])

        ple_gate = jax.nn.sigmoid(rms_norm(x, ple_norm_w[i]) @ w_ple_gate[i])
        x = x + ple_gate * (p[i] @ w_ple_proj[i])
    return rms_norm(x, final_norm_w)


_drawn_inputs = setup_inputs


def setup_inputs(seed=0):
    import zlib

    import numpy as np

    out = dict(_drawn_inputs(seed))
    spreads = {}
    factors = {'b_up': 8.0, 'b_down': 8.0, 'ple_norm_w': 45.428, 'final_norm_w': 7.501}
    for name, (base, spread) in spreads.items():
        noise = np.random.default_rng([zlib.crc32(name.encode()), seed]).standard_normal(out[name].shape)
        drawn = base * np.exp(spread * noise) if base else spread * noise
        out[name] = __import__('jax').numpy.asarray(drawn.astype(out[name].dtype))
    for name, factor in factors.items():
        out[name] = (out[name] * factor).astype(out[name].dtype)
    return out
```

```python
from contextlib import ExitStack

import concourse.bass as bass
from concourse import mybir

F32 = mybir.dt.float32
F32R = mybir.dt.float32r
BF16 = mybir.dt.bfloat16
U32 = mybir.dt.uint32
I32 = mybir.dt.int32
ALU = mybir.AluOpType
ACT = mybir.ActivationFunctionType
AX = mybir.AxisListType.X
ds = bass.ds

P = 128
SEQ, D = 512, 1024
TT = SEQ // P
KT = D // P
PLE = 256
EPS = 1e-6

HEADS, DK, DV = 8, 64, 128
LAMBDA_INIT = 0.2
QK_SCALE = DK ** -0.5
MASKED = -1e30

SSD_IN, SH, GROUPS, HG, HD, NST = 2048, 32, 4, 8, 64, 128
GW = SSD_IN // GROUPS
GT = GW // P
TAPS = 4
CONV_TILES = (SSD_IN + 2 * GROUPS * NST) // P

Q_AT, K_AT, V_AT, Z_AT = 0, 1024, 2048, 3072
X_AT = Z_AT + SSD_IN
B_AT = X_AT + SSD_IN
C_AT = B_AT + GROUPS * NST
DT_AT = C_AT + GROUPS * NST
GA_AT = DT_AT + SH
GS_AT = GA_AT + D

EXPERTS, TOPK, FF = 32, 4, 1024
LIMIT, ALPHA = 7.0, 1.702
EXTRA = (SEQ * TOPK - EXPERTS) // P
BLOCKS = EXPERTS + EXTRA
HALF = FF // 2
UNITS = 4

ATANH = [1.0 / n for n in (17, 15, 13, 11, 9, 7, 5, 3)]


def kb(n):
    return n * 256


class Unit:

    def __init__(self, first, reg=0, per=2):
        self.slot = first % 2
        self.number = reg * per + first
        self.landings = (reg * (per // 2) + (first // 2 + 1)) * 16

    def before(self, n):
        return self.number - n


def attention_unit(j, h0, reg=0):
    return Unit(3 * h0 + j, reg, 6)


SSD_UNITS = 3 * HEADS
GATE_UNITS = SSD_UNITS + 10 * GROUPS
PLE_DONE = (3, 4, 6, 8)
MOE_UNITS = GATE_UNITS + 2 * KT


SCAN_AT, PROJ_AT, WS_AT, XN_AT, OALL_AT = 0, 46, 71, 110, 79
YST_AT, YAT_AT, MERGED_AT, WOUT_AT, GATES_AT = 95, 0, 16, 32, 64
H_AT, ZERO_AT, MOE_AT, ARENA = 87, 127, 97, 131


SSD_ORDER = [("x", 0), ("b", 0), ("z", 0), ("x", 1), ("c", 0), ("z", 1), ("x", 2), ("z", 2), ("x", 3), ("z", 3)]
QUARTER = [[0, 1, 2], [3, 4, 5], [6, 7], [8, 9]]
CONV_AT = {0: 0, 1: 1, 3: 2, 4: 3, 6: 4, 8: 5}
TURNS = 2 * TT + 1


def wait(eng, sem, value):
    if not isinstance(value, int) or value > 0:
        eng.wait_ge(sem, value)


def up_piece(b, k):
    return b * 16 + (MOE_UNITS + k - (0 if isinstance(b, int) and b in (0, EXPERTS) else 8))


def down_piece(b, k):
    return b * 16 + (MOE_UNITS + k + (8 if isinstance(b, int) and b in (EXPERTS - 1, BLOCKS - 1) else 16))


class Own:

    def __init__(self, eng, sem):
        self.eng, self.sem, self.base, self.n = eng, sem, 0, 0

    def mark(self, ins):
        ins.then_inc(self.sem, 1)
        self.n += 1

    def wait(self):
        self.eng.wait_ge(self.sem, self.base + self.n)

    def then(self, ins):
        self.mark(ins)
        self.wait()

    def round(self, i, first, per):
        self.saved = self.n
        self.base, self.per = (i - first) * per, per

    def rounds(self, trips):
        assert self.n - self.saved == self.per, (self.n - self.saved, self.per)
        self.n, self.base = self.saved + trips * self.per, 0


def build(nc, x, p, mix_norm_w, w_in, lambda_q1, lambda_k1, lambda_q2, lambda_k2, da_head_norm_w,
          w_attn_branch, conv_w, conv_b, dt_bias, a_log, d_skip, ssd_norm_w, w_ssd_branch, w_out,
          moe_norm_w, router_w, router_b, w_up, b_up, w_down, b_down, ple_norm_w, w_ple_gate,
          w_ple_proj, final_norm_w, out):
    with ExitStack() as ctx:
        def sb(name, shape, dtype=F32):
            return ctx.enter_context(nc.sbuf_tensor(name, shape, dtype))

        def sem(name):
            return ctx.enter_context(nc.semaphore(name))

        xs = sb("residual", [P, TT, D])
        h_hi, h_lo = sb("h_hi", [P, KT, SEQ], F32R), sb("h_lo", [P, KT, SEQ], F32R)
        w_hi, w_lo = sb("w_hi", [P, 2, KT, P], F32R), sb("w_lo", [P, 2, KT, P], F32R)
        wdt_hi, wdt_lo = sb("wdt_hi", [P, KT, SH], F32R), sb("wdt_lo", [P, KT, SH], F32R)
        arena = sb("arena", [P, kb(ARENA)])
        psum = ctx.enter_context(nc.psum_tensor("psum", [P, 8 * 512], F32))

        def at(offset, *shape, extra=0):
            n = 1
            for s in shape:
                n *= s
            o = kb(offset) + extra
            v = arena[:, o:o + n]
            if len(shape) == 2:
                return v.rearrange("p (a b) -> p a b", a=shape[0])
            if len(shape) == 3:
                return v.rearrange("p (a b c) -> p a b c", a=shape[0], b=shape[1])
            return v

        def h_tile_of(t):
            return h_tile[:, t % 2]

        def bank(b, n=512, start=0):
            return psum[:, b * 512 + start:b * 512 + start + n]

        ident, ones = sb("ident", [P, P]), sb("ones", [P, P])
        upto = sb("upto", [P, P])
        after = sb("after", [P, P])
        before = sb("before", [P, P])
        negdist = at(24, SEQ)
        slopes = sb("slopes", [P, HEADS])
        eps = sb("eps", [P, 1])
        iota_e, iota_row = sb("iota_e", [P, EXPERTS]), sb("iota_row", [P, EXPERTS])
        iota_far = sb("iota_far", [P, EXPERTS])
        token_id = sb("token_id", [P, TT])
        extra_id = sb("extra_id", [1, EXTRA])
        ones_bf = sb("ones_bf", [P, P], BF16)

        NORMS = 3 * KT + SSD_IN // P + 1 + CONV_TILES
        par = sb("par", [P, NORMS])
        conv_col = sb("conv_col", [P, TAPS, CONV_TILES])
        par_mix, par_moe, par_ple = par[:, 0:KT], par[:, KT:2 * KT], par[:, 2 * KT:3 * KT]
        par_ssd = par[:, 3 * KT:3 * KT + 16]
        par_head = par[:, 3 * KT + 16:3 * KT + 17]
        par_convb = par[:, 3 * KT + 17:NORMS]
        byhead = sb("byhead", [P, 4, SH])
        lam = sb("lam", [P, 6])
        stat = sb("stat", [P, 3 * TT + TT, 2])

        ostat = sb("ostat", [P, 2, TT * HEADS])

        dt = sb("dt", [P, TT, SH])
        dta = sb("dta", [P, TT, SH])
        decay = sb("decay", [P, TT, 3, SH])
        gdt, gdta = sb("gdt", [P, TT, HG]), sb("gdta", [P, TT, HG])
        gdecay = sb("gdecay", [P, TT, 3, HG])
        gskip, gnorm = sb("gskip", [P, HG]), sb("gnorm", [P, GT])
        gconv, gconvb = sb("gconv", [P, TAPS, GT + 2]), sb("gconvb", [P, GT + 2])
        small = sb("small", [P, 24])

        gate_tab, slot_token = sb("gate_tab", [P, BLOCKS]), sb("slot_token", [P, BLOCKS], U32)
        block_token = sb("block_token", [P, 1], U32)
        rows_u = sb("rows_u", [P, TT * TOPK], U32)
        control = sb("control", [1, EXTRA + 1], I32)

        slots_dram = nc.dram_tensor("slots_dram", [BLOCKS * P, 2], F32).ap()
        h2_dram = nc.dram_tensor("h2_dram", [SEQ, D], F32).ap()
        y_dram = nc.dram_tensor("y_dram", [BLOCKS * P, D], F32).ap()
        bup_dram = nc.dram_tensor("bup_dram", [3, EXPERTS * 2 * FF], BF16).ap()
        bdn_dram = nc.dram_tensor("bdn_dram", [3, EXPERTS * D], BF16).ap()

        rows_a = at(PROJ_AT, P)
        rows_b = at(PROJ_AT, P, extra=P)
        lambdas = at(PROJ_AT, 4, DK, extra=2 * P)
        lam_tmp = at(PROJ_AT, 2, DK, extra=4 * P)
        NB = EXPERTS * 3 * FF // P
        bias_src = at(PROJ_AT, NB, extra=6 * P)
        bias_rest = at(PROJ_AT, NB, extra=12 * P)
        bias_part = at(PROJ_AT, 3 * NB // 2, extra=18 * P).bitcast(BF16).rearrange("p (a n) -> p a n", a=3)
        zero_slots = at(PROJ_AT, 2 * BLOCKS, extra=28 * P)
        w_dt = at(PROJ_AT, KT, SH, extra=29 * P)
        dt_work = at(PROJ_AT, 8, TT * SH, extra=31 * P)
        zero_rows = at(ZERO_AT, D)
        h_tile = at(H_AT, 2, KT, P)
        square_dump = at(WS_AT - 4, D)
        xn = at(XN_AT, 2, D)

        qT, kT = at(SCAN_AT, SEQ), at(SCAN_AT, SEQ, extra=SEQ)
        v_sb = at(SCAN_AT, TT, DV, extra=2 * SEQ)
        vT = at(SCAN_AT, SEQ, extra=11 * SEQ)
        dtT = vT[0:SH]
        score_at = [P * q * (q + 1) for q in range(TT)]
        probs = at(SCAN_AT, P * TT * (TT + 1), extra=3 * SEQ)
        atT = at(SCAN_AT, P * TT * (TT + 1) // 2, extra=3 * SEQ + P * TT * (TT + 1))
        amax, asum = small[:, 0:8], small[:, 8:16]
        arec = small[:, 16:24]
        o_all = arena[:, kb(OALL_AT):kb(OALL_AT) + SEQ * HEADS].rearrange(
            "p (q h d) -> p q h d", q=TT, h=HEADS)
        w_raw = [at(WS_AT + 4 * i, KT, P) for i in range(2)]
        yaT = at(YAT_AT, HEADS, SEQ)

        BT, CT = at(SCAN_AT, SEQ), at(SCAN_AT, SEQ, extra=SEQ)
        b_tok = at(SCAN_AT, TT, NST, extra=2 * SEQ)
        x_tok = at(SCAN_AT, TT, GW, extra=3 * SEQ)
        z_act = at(SCAN_AT, TT, GW, extra=7 * SEQ)
        y_tok = at(SCAN_AT, TT, GW, extra=11 * SEQ)
        dta_after = at(SCAN_AT, HG, P, extra=15 * SEQ)
        seg = at(SCAN_AT, HG, P, extra=17 * SEQ)
        xdt, xdte = at(SCAN_AT, GW, extra=19 * SEQ), at(SCAN_AT, GW, extra=20 * SEQ)
        state = at(SCAN_AT, GW, extra=21 * SEQ)
        y_tmp = at(SCAN_AT, GW, extra=22 * SEQ)
        RAW = SEQ + TAPS - 1
        raw = at(PROJ_AT, 2, RAW)
        pre = at(PROJ_AT, 2 * GT + 2, SEQ, extra=2 * RAW)
        cb = sb("cb", [P, P])
        ysT = at(YST_AT, SSD_IN // P, SEQ)

        w_ya, w_ys = at(WS_AT + 8, KT, P), at(WS_AT + 12, SSD_IN // P, P)
        mergedT = at(MERGED_AT, KT, SEQ)
        gate_a, gate_s, part_a = (at(GATES_AT + 2 * i, SEQ) for i in range(3))
        w_o = at(WOUT_AT, KT, D)

        RT = MOE_AT
        w_r = at(RT, KT, EXPERTS)
        logits = at(RT, TT, EXPERTS, extra=2 * P)
        top8 = at(RT, TT, 8, extra=3 * P)
        top8_at = arena[:, kb(RT) + 3 * P + 32:kb(RT) + 3 * P + 64].bitcast(U32).rearrange("p (a b) -> p a b", a=TT)
        top_idx = at(RT, TT * TOPK, extra=3 * P + 64)
        top_exp = at(RT, TT, TOPK, extra=3 * P + 80)
        top_sum = at(RT, 8, extra=3 * P + 96)
        onehot = at(RT, TT * TOPK, EXPERTS, extra=4 * P)
        chosen = at(RT, TT, EXPERTS, extra=8 * P)
        row_of = at(RT, TT, EXPERTS, extra=9 * P)
        far = at(RT, TT, EXPERTS, extra=10 * P)
        count = at(RT, 6, EXPERTS, extra=11 * P)
        picked = at(RT, TT * TOPK, EXPERTS, extra=13 * P)
        row_f = at(RT, TT * TOPK, extra=17 * P)
        slot_info = at(RT, TT * TOPK, 2, extra=17 * P + 16)
        ended = at(RT, EXTRA, EXPERTS, extra=18 * P)
        owner = at(RT, 16, extra=22 * P)
        slot_rows = at(RT, P, 2, extra=22 * P + 16)

        w_unit_up = [[arena[:, kb(32 * h + 8 * c):kb(32 * h + 8 * c + 8)].rearrange(
            "p (j u n) -> p j u n", j=2, u=2) for c in range(UNITS)] for h in range(2)]
        w_unit_dn = [at(64 + 8 * c, 2, D) for c in range(UNITS)]
        piece_hi, piece_lo = ([h[:, 2 * s:2 * s + 2, :] for s in range(4)] for h in (h_hi, h_lo))
        up_rows = [w_unit_up[1][k // 2][:, k % 2] for k in range(KT)]
        down_rows = [w_unit_dn[k // 2][:, k % 2, :].rearrange("p (n c) -> p n c", n=2) for k in range(KT)]
        act_hi, act_lo = w_hi[:, 0], w_lo[:, 0]
        x_hi, x_lo = w_hi[:, 1], w_lo[:, 1]
        xg, xgT = at(MOE_AT, D), at(MOE_AT + 4, KT, P)
        hidden = at(MOE_AT + 8, FF)
        y_out = at(MOE_AT + 16, D)
        g_sb, u_sb, sig_sb, t_sb = (at(MOE_AT + 20 + 2 * i, HALF) for i in range(4))
        bias_up = at(MOE_AT + 28, FF).bitcast(BF16)
        bias_dn = at(MOE_AT + 32, D // 2).bitcast(BF16)

        w_pg, p_sb, w_pp, final_w = at(0, KT, D), at(32, TT, PLE), at(36, 2, D), at(44, D)
        y_got = at(48, 4, D)
        h3T, pT = at(64, KT, SEQ), at(80, 2, SEQ)
        ple_gate, out_tile = at(84, D), at(88, 2, D)
        xn_ple = at(MOE_AT, 2, D)
        square_ple = at(MOE_AT + 8, D)

        x_landed = [sem(f"x_landed{t}") for t in range(TT)]
        params_landed, biases_landed, w_dt_landed = sem("params_landed"), sem("biases_landed"), sem("w_dt_landed")
        consts_ready, pool_own, dve_own, act_own = sem("consts_ready"), sem("pool_own"), sem("dve_own"), sem("act_own")
        params_turned = sem("params_turned")
        bias_parts_ready, bias_stored, slots_zeroed = sem("bias_parts_ready"), sem("bias_stored"), sem("slots_zeroed")
        zero_ready, y_zeroed = sem("zero_ready"), sem("y_zeroed")
        norm_rooted, xn_ready, xn_turned, h_ready = sem("norm_rooted"), sem("xn_ready"), sem("xn_turned"), sem("h_ready")
        dt_projected, dt_exp_asked, dt_exp_ready = sem("dt_projected"), sem("dt_exp_asked"), sem("dt_exp_ready")
        dta_ready, decay_summed, decay_ready = sem("dta_ready"), sem("decay_summed"), sem("decay_ready")
        lam_asked, lam_exp_ready = sem("lam_asked"), sem("lam_exp_ready")
        unit_landed = [sem(f"unit_landed{i}") for i in range(2)]
        hi_ready, lo_ready, unit_used = sem("hi_ready"), sem("lo_ready"), sem("unit_used")
        h_hi_ready, h_lo_ready, wdt_split = sem("h_hi_ready"), sem("h_lo_ready"), sem("wdt_split")
        q_copied, k_copied, v_copied = sem("q_copied"), sem("k_copied"), sem("v_copied")
        vt_copied, v_turned, dtt_copied = sem("vt_copied"), sem("v_turned"), sem("dtt_copied")
        scores_done, scores_drained, max_ready = sem("scores_done"), sem("scores_drained"), sem("max_ready")
        probs_ready, attn_ready, attn_turned = sem("probs_ready"), sem("attn_ready"), sem("attn_turned")
        at_copied, pv_done = sem("at_copied"), sem("pv_done")
        o_squared, o_rooted, o_ready, o_turned, ya_ready = (
            sem("o_squared"), sem("o_rooted"), sem("o_ready"), sem("o_turned"), sem("ya_ready"))
        proj_copied, conv_done = sem("proj_copied"), sem("conv_done")
        silu_done, chunk_turned, chunk_copied = sem("silu_done"), sem("chunk_turned"), sem("chunk_copied")
        scan_params_ready = sem("scan_params_ready")
        dta_after_ready, cb_done, seg_summed, seg_ready = (
            sem("dta_after_ready"), sem("cb_done"), sem("seg_summed"), sem("seg_ready"))
        xdte_ready, mix_ready, y_diag_done, y_off_done = (
            sem("xdte_ready"), sem("mix_ready"), sem("y_diag_done"), sem("y_off_done"))
        state_summed, state_ready, cb_read = sem("state_summed"), sem("state_ready"), sem("cb_read")
        y_drained = sem("y_drained")
        y_gated, y_rooted, y_normed, y_turned, ys_ready = (
            sem("y_gated"), sem("y_rooted"), sem("y_normed"), sem("y_turned"), sem("ys_ready"))
        w_mg_landed = [sem(f"w_mg_landed{i}") for i in range(2)]
        mg_projected, gates_ready, mg_read = sem("mg_projected"), sem("gates_ready"), sem("mg_read")
        w_o_landed, w_r_landed = sem("w_o_landed"), sem("w_r_landed")
        out_projected, x1_ready = sem("out_projected"), sem("x1_ready")
        h2_stored = [sem(f"h2_stored{t}") for t in range(TT)]
        routed, logits_read, chosen_ready, ranked = (
            sem("routed"), sem("logits_read"), sem("chosen_ready"), sem("ranked"))
        top_asked, top_exp_ready, slots_ready = sem("top_asked"), sem("top_exp_ready"), sem("slots_ready")
        slots_stored, slot_rows_landed, slots_turned, tables_ready = (
            sem("slots_stored"), sem("slot_rows_landed"), sem("slots_turned"), sem("tables_ready"))
        bias_cleared, gather_cleared = sem("bias_cleared"), sem("gather_cleared")

        (block_token_ready, xg_landed, x_turned, xt_ready, up_used, up_done, g_ready, sig_ready, hidden_own,
         act_ready, act_turned, actt_ready, act_hi_ready, x_hi_ready, x_lo_ready, down_done, y_ready, y_stored, bias_up_landed,
         bias_dn_landed) = (sem(n) for n in (
            "block_token_ready", "xg_landed", "x_turned", "xt_ready", "up_used", "up_done",
            "g_ready", "sig_ready", "hidden_own", "act_ready", "act_turned", "actt_ready",
            "act_hi_ready", "x_hi_ready", "x_lo_ready", "down_done", "y_ready", "y_stored", "bias_up_landed", "bias_dn_landed"))
        w_up_landed = [[sem(f"w_up_landed{h}{c}") for c in range(UNITS)] for h in range(2)]
        w_dn_landed = [sem(f"w_dn_landed{c}") for c in range(UNITS)]
        w_pg_landed, ple_in_landed = sem("w_pg_landed"), sem("ple_in_landed")
        y_got_landed = [sem(f"y_got_landed{b}") for b in range(4)]
        y_got_added = sem("y_got_added")
        p_turned, p_ready = sem("p_turned"), sem("p_ready")
        ple_projected, ple_sig_ready, ple_added = sem("ple_projected"), sem("ple_sig_ready"), sem("ple_added")
        end_rooted, out_ready = sem("end_rooted"), sem("out_ready")
        out_stored = [sem(f"out_stored{b}") for b in range(2)]

        x_d, out_d, p_d = x[0], out[0], p[0, 0]
        w_in_d = w_in[0].rearrange("(k p) n -> p k n", p=P)
        w_ya_d = w_attn_branch[0].rearrange("(k p) n -> p k n", p=P)
        w_ys_d = w_ssd_branch[0].rearrange("(k p) n -> p k n", p=P)
        w_o_d = w_out[0].rearrange("(k p) n -> p k n", p=P)
        w_up_d = w_up[0].rearrange("e (c j p) (u h n) -> e h c p j u n", j=2, p=P, u=2, h=2)
        w_dn_d = w_down[0].rearrange("e (c j p) n -> e c p j n", j=2, p=P)

        PARAM_DMAS = 15
        block = ctx.enter_context(nc.Block())

        @block.sync
        def _(sp):
            for t in range(TT):
                sp.dma_start(xs[:, t, :], x_d[t * P:(t + 1) * P, :]).then_inc(x_landed[t], 16)

            sp.dma_start(w_dt, w_in_d[:, :, DT_AT:DT_AT + SH]).then_inc(w_dt_landed, 16)

            def load_unit(unit, column):
                if not isinstance(column, int):
                    column = sp.snap(column)
                wait(sp, lo_ready, unit.before(1))
                sp.dma_start(w_raw[unit.slot], w_in_d[:, :, ds(column, P)]).then_inc(unit_landed[unit.slot], 16)

            def load_heads(reg):
                for h0 in range(2):
                    for j, start in enumerate((Q_AT, K_AT, V_AT)):
                        load_unit(attention_unit(j, h0, reg), reg * (2 * P) + (start + P * h0))

            load_heads(0)
            with sp.Fori(1, HEADS // 2) as i:
                load_heads(i)
            sp.wait_ge(zero_ready, 1)
            sp.dma_start(y_dram[EXPERTS * P:].rearrange("(b p) n -> p b n", p=P),
                         zero_rows.unsqueeze(1).broadcast_to([P, EXTRA, D])).then_inc(y_zeroed, 16)
            with sp.Fori(0, GROUPS) as g:
                for n, (kind, i) in enumerate(SSD_ORDER):
                    start, width = {"x": (X_AT, GW), "z": (Z_AT, GW), "b": (B_AT, P), "c": (C_AT, P)}[kind]
                    load_unit(Unit(SSD_UNITS + n, g, 10), g * width + (start + P * i))

            def load_gates(d):
                load_unit(Unit(GATE_UNITS, d), d * P + GA_AT)
                load_unit(Unit(GATE_UNITS + 1, d), d * P + GS_AT)

            def load_merge(d):
                for i, (dst, src) in enumerate(((w_ya, w_ya_d), (w_ys, w_ys_d))):
                    wait(sp, mg_projected, 2 * (d - 1) + i + 1)
                    sp.dma_start(dst, src[:, :, ds(P * d, P)]).then_inc(w_mg_landed[i], 16)

            load_gates(0)
            load_gates(1)
            sp.wait_ge(o_turned, TT)
            load_merge(0)
            sp.wait_ge(y_turned, TT * GROUPS)
            for half in range(2):
                sp.dma_start(w_o[:, :, half * 512:half * 512 + 512],
                             w_o_d[:, :, half * 512:half * 512 + 512]).then_inc(w_o_landed, 16)
            with sp.Fori(1, KT - 1) as d:
                load_merge(d)
                load_gates(d + 1)
            load_merge(KT - 1)

            def load_up(i, half, expert):
                for c in range(UNITS):
                    if half == 0:
                        wait(sp, up_used, UNITS * (i - 1) + c + 1)
                    elif not isinstance(i, int) or i:
                        sp.wait_ge(lo_ready, up_piece(i - 1, 2 * c + 1) + 1)
                    for j in range(2):
                        sp.dma_start(w_unit_up[half][c][:, j],
                                     w_up_d[ds(expert, 1), half, c, :, j].rearrange("a p u n -> (a p) u n")
                                     ).then_inc(w_up_landed[half][c], 16)

            def load_bias_up(i, expert):
                wait(sp, up_done, 2 * i)
                sp.dma_start(bias_up[0:3, :], bup_dram[:, ds(expert * (2 * FF), 2 * FF)]
                             ).then_inc(bias_up_landed, 16)

            def load_down(i, expert):
                for c in range(UNITS):
                    if not isinstance(i, int) or i:
                        sp.wait_ge(lo_ready, down_piece(i - 1, 2 * c + 1) + 1)
                    sp.dma_start(w_unit_dn[c], w_dn_d[ds(expert, 1), c].rearrange("a p j n -> (a p) j n")
                                 ).then_inc(w_dn_landed[c], 16)
                wait(sp, down_done, i)
                sp.dma_start(bias_dn[0:3, :], bdn_dram[:, ds(expert * D, D)]
                             ).then_inc(bias_dn_landed, 16)

            sp.wait_ge(mg_projected, 2 * KT)
            sp.dma_start(w_r, router_w[0].rearrange("(k p) n -> p k n", p=P)).then_inc(w_r_landed, 16)
            sp.wait_ge(out_projected, TT)
            load_up(0, 0, 0)
            load_up(0, 1, 0)
            sp.wait_ge(slots_stored, 16 * TT * TOPK)
            sp.dma_start(slot_rows[0:BLOCKS], slots_dram.rearrange("(b s) two -> b s two", s=P)
                         ).then_inc(slot_rows_landed, 16)
            sp.wait_ge(bias_stored, 16 * 6)
            sp.wait_ge(bias_cleared, 1)
            load_bias_up(0, 0)
            load_up(1, 0, 1)
            load_up(1, 1, 1)
            load_bias_up(1, 1)
            load_down(0, 0)
            with sp.Fori(2, EXPERTS) as i:
                load_up(i, 0, i)
                load_up(i, 1, i)
                load_bias_up(i, i)
                load_down(i - 1, i - 1)
            load_down(EXPERTS - 1, EXPERTS - 1)

            extra = sp.value_load(control[0:1, EXTRA:EXTRA + 1], min_val=0, max_val=EXTRA)
            with sp.If(extra > 0):
                def owner_of(b):
                    return sp.value_load(control[0:1, ds(b, 1)], min_val=0, max_val=EXPERTS - 1)

                for b in range(2):
                    e = owner_of(b)
                    load_up(EXPERTS + b, 0, e)
                    load_up(EXPERTS + b, 1, e)
                    load_bias_up(EXPERTS + b, e)
                load_down(EXPERTS, owner_of(0))
                with sp.Fori(2, EXTRA) as b:
                    e = owner_of(b)
                    load_up(b + EXPERTS, 0, e)
                    load_up(b + EXPERTS, 1, e)
                    load_bias_up(b + EXPERTS, e)
                    load_down(b + (EXPERTS - 1), owner_of(b - 1))
                load_down(BLOCKS - 1, owner_of(EXTRA - 1))

            sp.wait_ge(up_done, 2 * EXPERTS)
            with sp.If(extra > 0):
                sp.wait_ge(up_done, 2 * BLOCKS)
            sp.dma_start(w_pg, w_ple_gate[0].rearrange("(k p) n -> p k n", p=P)).then_inc(w_pg_landed, 16)
            sp.dma_start(p_sb, p_d.rearrange("(t p) n -> p t n", p=P)).then_inc(ple_in_landed, 16)
            sp.dma_start(w_pp, w_ple_proj[0].rearrange("(k p) n -> p k n", p=P)).then_inc(ple_in_landed, 16)
            sp.dma_start(final_w, final_norm_w.partition_broadcast(P)).then_inc(ple_in_landed, 16)
            for t in range(TT):
                sp.wait_ge(out_ready, t + 1)
                sp.dma_start(out_d[t * P:(t + 1) * P, :], out_tile[:, t % 2, :]).then_inc(out_stored[t % 2], 16)
            for b in range(2):
                sp.wait_ge(out_stored[b], 16 * TT // 2)

        @block.gpsimd
        def _(pool):
            own = Own(pool, pool_own)
            own.mark(pool.memset(ident[:], 0.0))
            for m in (upto, after, before):
                own.mark(pool.memset(m[:], 1.0))
            own.wait()
            pool.affine_select(out=ident[:], in_=ident[:], compare_op=ALU.not_equal, fill=1.0, base=0,
                               pattern=[[-1, P]], channel_multiplier=1)
            pool.affine_select(out=upto[:], in_=upto[:], compare_op=ALU.is_ge, fill=0.0, base=0,
                               pattern=[[1, P]], channel_multiplier=-1)
            pool.affine_select(out=after[:], in_=after[:], compare_op=ALU.is_gt, fill=0.0, base=0,
                               pattern=[[-1, P]], channel_multiplier=1)
            pool.affine_select(out=before[:], in_=before[:], compare_op=ALU.is_gt, fill=0.0, base=0,
                               pattern=[[1, P]], channel_multiplier=-1)
            pool.memset(ones[:], 1.0)
            pool.memset(ones_bf[:], 1.0)
            pool.memset(eps[:], EPS)
            for h in range(HEADS):
                pool.memset(slopes[:, h:h + 1], 2.0 ** (-8.0 * (h + 1) / HEADS))
            pool.iota(negdist, [[1, SEQ]], base=P - SEQ, channel_multiplier=-1,
                      allow_small_or_imprecise_dtypes=True)
            pool.iota(iota_e[:], [[1, EXPERTS]], base=0, channel_multiplier=0,
                      allow_small_or_imprecise_dtypes=True)
            pool.iota(iota_row[:], [[P, EXPERTS]], base=0, channel_multiplier=0,
                      allow_small_or_imprecise_dtypes=True)
            pool.iota(iota_far[:], [[-P, EXPERTS]], base=P * (EXPERTS - 1), channel_multiplier=0,
                      allow_small_or_imprecise_dtypes=True)
            pool.iota(token_id[:], [[P, TT]], base=0, channel_multiplier=1,
                      allow_small_or_imprecise_dtypes=True)
            pool.iota(extra_id[:], [[1, EXTRA]], base=0, channel_multiplier=0,
                      allow_small_or_imprecise_dtypes=True).then_inc(consts_ready, 1)

            def masks(g, c):
                if c == 0:
                    pool.wait_ge(scan_params_ready, g + 1)
                wait(pool, seg_summed, TT * g + c)
                pool.tensor_tensor(dta_after, after[:].unsqueeze(1).broadcast_to([P, HG, P]),
                                   gdta[:, c, :].unsqueeze(2).broadcast_to([P, HG, P]),
                                   ALU.mult).then_inc(dta_after_ready, 1)

            for c in range(TT):
                masks(0, c)
            with pool.Fori(1, GROUPS) as g:
                for c in range(TT):
                    masks(g, c)

            pool.wait_ge(slots_zeroed, 16)
            pool.wait_ge(slots_ready, 1)
            for j in range(TT * TOPK):
                pool.indirect_dma_start(slots_dram, bass.IndirectOffsetOnAxis(rows_u[:, j:j + 1], 0),
                                        slot_info[:, j, :], None).then_inc(slots_stored, 16)

            def fetch(b):
                wait(pool, xg_landed, 16 * b)
                pool.tensor_copy(block_token[:], slot_token[:, ds(b, 1)]).then_inc(block_token_ready, 1)
                pool.wait_ge(block_token_ready, b + 1)
                wait(pool, x_turned, b)
                pool.sem_inc(gather_cleared, 1)
                pool.indirect_dma_start(xg, None, h2_dram, bass.IndirectOffsetOnAxis(block_token[:], 0)
                                        ).then_inc(xg_landed, 16)

            pool.wait_ge(tables_ready, 1)
            for t in range(TT):
                pool.wait_ge(h2_stored[t], 16)
            fetch(0)
            with pool.Fori(1, EXPERTS) as b:
                fetch(b)
            pool.wait_ge(y_stored, 16 * EXPERTS)
            extra = pool.value_load(control[0:1, EXTRA:EXTRA + 1], min_val=0, max_val=EXTRA)
            with pool.If(extra > 0):
                pool.wait_ge(y_zeroed, 16)
                with pool.Fori(EXPERTS, BLOCKS) as b:
                    fetch(b)
                pool.wait_ge(y_stored, 16 * BLOCKS)

            pool.wait_ge(y_zeroed, 16)
            for n in range(TT * TOPK):
                wait(pool, y_got_added, n - 3)
                pool.indirect_dma_start(y_got[:, n % 4, :], None, y_dram,
                                        bass.IndirectOffsetOnAxis(rows_u[:, n:n + 1], 0)
                                        ).then_inc(y_got_landed[n % 4], 16)

        @block.scalar
        def _(act):
            own = Own(act, act_own)
            row = 0
            for src in (mix_norm_w[0], moe_norm_w[0], ple_norm_w[0], ssd_norm_w[0], da_head_norm_w[0], conv_b[0]):
                n = src.shape[0] // P
                act.dma_start(rows_a[row:row + n, :], src.rearrange("(r c) -> r c", c=P)
                              ).then_inc(params_landed, 16)
                row += n
            act.dma_start(rows_b[0:TAPS * CONV_TILES, :], conv_w[0].rearrange("k (t c) -> (k t) c", c=P)
                          ).then_inc(params_landed, 16)
            for i, src in enumerate((dt_bias[0], a_log[0], d_skip[0], router_b[0])):
                act.dma_start(byhead[:, i, :], src.partition_broadcast(P)).then_inc(params_landed, 16)
            for i, src in enumerate((lambda_q1[0], lambda_k1[0], lambda_q2[0], lambda_k2[0])):
                act.dma_start(lambdas[:, i, :], src.partition_broadcast(P)).then_inc(params_landed, 16)
            act.dma_start(bias_src[:, 0:512], b_up[0].rearrange("e n -> (e n)").rearrange("(p n) -> p n", p=P)
                          ).then_inc(biases_landed, 16)
            act.dma_start(bias_src[:, 512:NB], b_down[0].rearrange("e n -> (e n)").rearrange("(p n) -> p n", p=P)
                          ).then_inc(biases_landed, 16)

            def root_mean(stage, t, src, ready, n, dump):
                ready()
                own.then(act.activation(dump, src, ACT.Square, accum_out=stat[:, TT * stage + t, 0:1]))
                act.activation(stat[:, TT * stage + t, 1:2], stat[:, TT * stage + t, 0:1], ACT.Sqrt,
                               bias=eps[:], scale=1.0 / n).then_inc(norm_rooted, 1)

            act.wait_ge(consts_ready, 1)
            for t in range(TT):
                root_mean(0, t, xs[:, t, :], lambda: act.wait_ge(x_landed[t], 16), D, square_dump)

            act.wait_ge(zero_ready, 1)
            act.dma_start(slots_dram.rearrange("(p n) two -> p (n two)", p=P), zero_slots
                          ).then_inc(slots_zeroed, 16)

            def split_h(t):
                act.wait_ge(h_ready, t + 1)
                act.activation(h_hi[:, :, t * P:(t + 1) * P], h_tile_of(t), ACT.Copy).then_inc(h_hi_ready, 1)

            def split(unit):
                act.wait_ge(unit_landed[unit.slot], unit.landings)
                wait(act, unit_used, unit.before(1))
                act.activation(w_hi[:, unit.slot], w_raw[unit.slot], ACT.Copy).then_inc(hi_ready, 1)

            act.wait_ge(w_dt_landed, 16)
            act.activation(wdt_hi[:], w_dt, ACT.Copy).then_inc(wdt_split, 1)
            split(Unit(0))
            split(Unit(1))
            for t in range(TT):
                split_h(t)
            act.wait_ge(bias_parts_ready, 1)
            for i in range(3):
                act.dma_start(bup_dram[i].rearrange("(p n) -> p n", p=P), bias_part[:, i, 0:512]
                              ).then_inc(bias_stored, 16)
                act.dma_start(bdn_dram[i].rearrange("(p n) -> p n", p=P), bias_part[:, i, 512:NB]
                              ).then_inc(bias_stored, 16)

            act.wait_ge(lam_asked, 1)
            act.activation(lam[:, 2:4], lam[:, 0:2], ACT.Exp).then_inc(lam_exp_ready, 1)
            act.wait_ge(params_landed, 16 * PARAM_DMAS)
            own.mark(act.activation(byhead[:, 1, :], byhead[:, 1, :], ACT.Exp))
            act.wait_ge(dt_exp_asked, 1)
            act.activation(dt_work[:, 2, :], dt_work[:, 1, :], ACT.Exp).then_inc(dt_exp_ready, 1)

            def attention(h0, reg=0, first=False, last=False):
                h = reg * 2 + h0
                if not last:
                    act.wait_ge(unit_used, attention_unit(0, h0, reg).number + 1)
                    act.activation(qT, bank(0), ACT.Copy, scale=QK_SCALE).then_inc(q_copied, 1)
                    split(attention_unit(2, h0, reg))
                if not first:
                    act.wait_ge(attn_turned, h)
                    act.activation(atT, psum[:, 3 * 512:3 * 512 + P * 10], ACT.Copy).then_inc(at_copied, 1)
                if not last:
                    split(attention_unit(3, h0, reg))
                    split(attention_unit(4, h0, reg))
                    act.wait_ge(unit_used, attention_unit(2, h0, reg).number + 1)
                    act.activation(vT, bank(6), ACT.Copy).then_inc(vt_copied, 1)
                    act.wait_ge(v_turned, h + 1)
                    wait(act, pv_done, h)
                    act.activation(v_sb.rearrange("p t d -> p (t d)"), bank(2), ACT.Copy).then_inc(v_copied, 1)
                    for q in range(TT):
                        act.wait_ge(max_ready, h * TT + q + 1)
                        w = P * (q + 1)
                        for m in range(2):
                            s = probs[:, score_at[q] + m * w:score_at[q] + m * w + w]
                            ins = act.activation(s, s, ACT.Exp, bias=amax[:, 2 * q + m:2 * q + m + 1],
                                                 accum_out=asum[:, 2 * q + m:2 * q + m + 1])
                        ins.then_inc(probs_ready, 1)

            attention(0, first=True)
            with act.Fori(0, HEADS // 2 - 1) as i:
                attention(1, i)
                attention(2, i)
            attention(HEADS - 1)
            attention(HEADS, last=True)

            act.wait_ge(decay_summed, 1)
            act.activation(decay[:].rearrange("p c k h -> p (c k h)"), bank(5, TT * 3 * SH), ACT.Exp
                           ).then_inc(decay_ready, 1)
            act.wait_ge(o_squared, 1)
            act.activation(ostat[:, 1, :], ostat[:, 0, :], ACT.Sqrt,
                           bias=eps[:], scale=1.0 / DV).then_inc(o_rooted, 1)

            def copy_tile(g, n):
                kind, i = SSD_ORDER[n]
                unit = Unit(SSD_UNITS + n, g, 10)
                act.wait_ge(unit_used, unit.number + 1)
                if kind == "z":
                    dst = pre[:, GT + 2 + i, :]
                else:
                    conv = CONV_AT[n]
                    wait(act, conv_done, 6 * g + conv - 1)
                    dst = raw[:, conv % 2, TAPS - 1:RAW]
                act.activation(dst, bank(n % 2), ACT.Copy).then_inc(proj_copied, 1)
                split(Unit(SSD_UNITS + n + 2, g, 10))

            def silus(g):
                act.wait_ge(conv_done, 6 * (g + 1))
                wait(act, y_gated, TT * g)
                wait(act, y_diag_done, TT * g)
                for i in range(GT):
                    act.activation(pre[:, i, :], pre[:, i, :], ACT.Silu).then_inc(silu_done, 1)
                act.activation(BT, pre[:, GT, :], ACT.Silu).then_inc(silu_done, 1)
                act.activation(CT, pre[:, GT + 1, :], ACT.Silu).then_inc(silu_done, 1)
                act.wait_ge(proj_copied, 10 * (g + 1))
                z = pre[:, GT + 2:2 * GT + 2, :]
                act.activation(z, z, ACT.Silu).then_inc(silu_done, 1)

            def chunk_copies(g):
                for c in range(TT):
                    act.wait_ge(chunk_turned, TURNS * g + c + 1)
                    act.activation(x_tok[:, c, :], bank(3 + c), ACT.Copy).then_inc(chunk_copied, 1)
                act.wait_ge(chunk_turned, TURNS * g + TT + 1)
                act.activation(b_tok.rearrange("p c n -> p (c n)"), bank(7), ACT.Copy).then_inc(chunk_copied, 1)
                for c in range(TT):
                    act.wait_ge(chunk_turned, TURNS * g + TT + 1 + c + 1)
                    act.activation(z_act[:, c, :], bank(3 + c), ACT.Copy).then_inc(chunk_copied, 1)

            def scan_chunk(g, c):
                act.wait_ge(seg_summed, TT * g + c + 1)
                act.activation(seg.rearrange("p r l -> p (r l)"), psum[:, 3 * 512:5 * 512], ACT.Exp
                               ).then_inc(seg_ready, 1)

            def roots(g):
                act.wait_ge(y_gated, TT * (g + 1))
                for c in range(TT):
                    own.mark(act.activation(pre[:, c, :], y_tok[:, c, :], ACT.Square,
                                            accum_out=small[:, c:c + 1]))
                own.wait()
                act.activation(small[:, 4:8], small[:, 0:4], ACT.Sqrt, bias=eps[:], scale=1.0 / GW
                               ).then_inc(y_rooted, 1)

            act.wait_ge(bias_stored, 16 * 6)
            act.wait_ge(slots_zeroed, 16)
            for n in range(10):
                copy_tile(0, n)
            silus(0)
            chunk_copies(0)
            with act.Fori(1, GROUPS) as g:
                own.round(g, 1, 4)
                for c in range(TT):
                    for n in QUARTER[c][:1]:
                        copy_tile(g, n)
                    scan_chunk(g - 1, c)
                    for n in QUARTER[c][1:]:
                        copy_tile(g, n)
                silus(g)
                chunk_copies(g)
                roots(g - 1)
            own.rounds(GROUPS - 1)
            for c in range(TT):
                scan_chunk(GROUPS - 1, c)
            roots(GROUPS - 1)

            def merge(d, last=False):
                for j, gate in enumerate((gate_a, gate_s)):
                    act.wait_ge(unit_used, Unit(GATE_UNITS + j, d).number + 1)
                    wait(act, mg_read, d)
                    act.activation(gate, bank(j), ACT.Sigmoid).then_inc(gates_ready, 1)
                    if not last:
                        split(Unit(GATE_UNITS + 2 + j, d))

            merge(0)
            with act.Fori(1, KT - 1) as d:
                merge(d)
            merge(KT - 1, last=True)

            def store_h2(t):
                act.wait_ge(xn_ready, TT + t + 1)
                act.dma_start(h2_dram[t * P:(t + 1) * P, :], xn[:, t % 2, :]).then_inc(h2_stored[t], 16)

            act.wait_ge(mg_read, KT)
            for t in range(TT):
                root_mean(1, t, xs[:, t, :], lambda: act.wait_ge(x1_ready, t + 1), D,
                          at(GATES_AT, D))
                if t:
                    store_h2(t - 1)
            store_h2(TT - 1)
            act.wait_ge(top_asked, TT)
            act.activation(top_exp, top_exp, ACT.Exp).then_inc(top_exp_ready, 1)

            def sigmoid_half(b, half):
                act.wait_ge(g_ready, 2 * b + half + 1)
                act.activation(sig_sb, g_sb, ACT.Sigmoid, scale=ALPHA).then_inc(sig_ready, 1)

            def expert_out(b):
                act.wait_ge(down_done, b + 1)
                if isinstance(b, int) and b == 0:
                    act.wait_ge(tables_ready, 1)
                wait(act, y_stored, 16 * b)
                act.activation(y_out, psum[:, 4 * 512:6 * 512], ACT.Copy, scale=gate_tab[:, ds(b, 1)]
                               ).then_inc(y_ready, 1)
                act.wait_ge(y_ready, b + 1)
                act.dma_start(y_dram[ds(b * P, P), :], y_out).then_inc(y_stored, 16)

            def split_act(b):
                act.wait_ge(act_turned, b + 1)
                act.activation(act_hi, psum[:, 6 * 512:8 * 512].rearrange("p (k t) -> p k t", t=P), ACT.Copy
                               ).then_inc(act_hi_ready, 1)

            def split_x(b):
                act.wait_ge(xt_ready, b + 1)
                act.activation(x_hi, xgT, ACT.Copy).then_inc(x_hi_ready, 1)

            def split_piece(number, slot, rows):
                act.wait_ge(unit_used, max(MOE_UNITS, number - 3) if isinstance(number, int) else number - 3)
                act.activation(piece_hi[slot], rows, ACT.Copy).then_inc(hi_ready, 1)

            def split_up(b, start):
                for k in range(start, start + 4):
                    act.wait_ge(w_up_landed[1][k // 2], 32 * (b + 1))
                    split_piece(up_piece(b, k), k % 4, up_rows[k])

            def split_down(b, start):
                for k in range(start, start + 4):
                    act.wait_ge(w_dn_landed[k // 2], 16 * (b + 1))
                    split_piece(down_piece(b, k), k % 4, down_rows[k])

            def round_of(b):
                split_x(b)
                split_up(b, 0)
                sigmoid_half(b, 0)
                split_up(b, 4)
                split_act(b - 1)
                split_down(b - 1, 0)
                sigmoid_half(b, 1)
                split_down(b - 1, 4)
                expert_out(b - 1)

            def experts(first, end):
                split_up(first, 0)
                split_x(first)
                sigmoid_half(first, 0)
                split_up(first, 4)
                sigmoid_half(first, 1)
                round_of(first + 1)
                with act.Fori(first + 2, end) as b:
                    round_of(b)
                split_act(end - 1)
                split_down(end - 1, 0)
                split_down(end - 1, 4)
                expert_out(end - 1)

            experts(0, EXPERTS)
            extra = act.value_load(control[0:1, EXTRA:EXTRA + 1], min_val=0, max_val=EXTRA)
            with act.If(extra > 0):
                experts(EXPERTS, BLOCKS)

            act.wait_ge(p_turned, 1)
            act.activation(pT.rearrange("p k t -> p (k t)"), psum[:, 6 * 512:8 * 512], ACT.Copy).then_inc(p_ready, 1)
            for t in range(TT):
                root_mean(2, t, xs[:, t, :], lambda: act.wait_ge(y_got_added, TOPK * (t + 1)), D, square_ple)
            for t in range(TT):
                act.wait_ge(ple_projected, PLE_DONE[t])
                wait(act, ple_added, t)
                act.activation(ple_gate, psum[:, 0:1024], ACT.Sigmoid).then_inc(ple_sig_ready, 1)
                act.wait_ge(ple_added, t + 1)
                own.then(act.activation(square_ple, xs[:, t, :], ACT.Square, accum_out=stat[:, 3 * TT + t, 0:1]))
                act.activation(stat[:, 3 * TT + t, 1:2], stat[:, 3 * TT + t, 0:1], ACT.Sqrt,
                               bias=eps[:], scale=1.0 / D).then_inc(end_rooted, 1)

        @block.vector
        def _(dve):
            own = Own(dve, dve_own)

            def split(unit):
                dve.wait_ge(hi_ready, unit.number + 1)
                dve.tensor_tensor(w_lo[:, unit.slot], w_raw[unit.slot], w_hi[:, unit.slot].bitcast(F32),
                                  ALU.subtract).then_inc(lo_ready, 1)

            dve.memset(zero_slots, 0.0)
            dve.memset(zero_rows, 0.0).then_inc(zero_ready, 1)
            dve.wait_ge(consts_ready, 1)
            own.mark(dve.scalar_tensor_tensor(out=negdist, in0=negdist, scalar=-1.0, in1=negdist,
                                              op0=ALU.mult, op1=ALU.min))

            own.wait()
            own.mark(dve.memset(negdist[0:64, SEQ - 64:SEQ], MASKED))

            def normalize(stage, t, buf):
                n = TT * stage + t
                dve.wait_ge(norm_rooted, n + 1)
                own.then(dve.reciprocal(stat[:, n, 0:1], stat[:, n, 1:2]))
                wait(dve, xn_turned, n - 1)
                if stage == 1 and t >= 2:
                    dve.wait_ge(h2_stored[t - 2], 16)
                dve.tensor_scalar(buf[:, t % 2, :], xs[:, t, :], stat[:, n, 0:1], None, ALU.mult
                                  ).then_inc(xn_ready, 1)

            def evacuate(stage, t, weights, dst):
                n = TT * stage + t
                dve.wait_ge(xn_turned, n + 1)
                if stage == 1 and t >= 2:
                    dve.wait_ge(routed, t - 1)
                dve.tensor_tensor(dst,
                                  psum[:, 4 * 512:6 * 512].rearrange("p (k t) -> p k t", t=P),
                                  weights.unsqueeze(2).broadcast_to([P, KT, P]), ALU.mult).then_inc(h_ready, 1)

            normalize(0, 0, xn)
            dve.wait_ge(params_turned, 1)
            dve.tensor_copy(par[:], bank(7, NORMS))
            own.then(dve.tensor_copy(conv_col[:].rearrange("p k t -> p (k t)"), bank(7, TAPS * CONV_TILES, P)))
            own.then(dve.tensor_scalar(par_head, par_head, 1.0 - LAMBDA_INIT, None, ALU.mult))
            def split_h(t):
                dve.wait_ge(h_hi_ready, t + 1)
                cols = slice(t * P, (t + 1) * P)
                dve.tensor_tensor(h_lo[:, :, cols], h_tile_of(t), h_hi[:, :, cols].bitcast(F32), ALU.subtract
                                  ).then_inc(h_lo_ready, 1)

            for t in range(TT):
                if t + 1 < TT:
                    normalize(0, t + 1, xn)
                if t >= 2:
                    split_h(t - 2)
                    dve.wait_ge(h_lo_ready, t - 1)
                evacuate(0, t, par_mix, h_tile_of(t))
            dve.wait_ge(wdt_split, 1)
            dve.tensor_tensor(wdt_lo[:], w_dt, wdt_hi[:].bitcast(F32), ALU.subtract).then_inc(wdt_split, 1)
            split(Unit(0))
            split_h(TT - 2)
            split_h(TT - 1)
            split(Unit(1))

            for m in range(2):
                ins = dve.tensor_tensor_reduce(out=lam_tmp[:, m, :], in0=lambdas[:, 2 * m, :],
                                               in1=lambdas[:, 2 * m + 1, :], scale=1.0, scalar=0.0, op0=ALU.mult,
                                               op1=ALU.add, accum_out=lam[:, m:m + 1])
            ins.then_inc(lam_asked, 1)

            dve.wait_ge(biases_landed, 32)
            own.then(dve.tensor_copy(bias_part[:, 0, :], bias_src))
            own.then(dve.tensor_tensor(bias_rest, bias_src, bias_part[:, 0, :], ALU.subtract))
            own.then(dve.tensor_copy(bias_part[:, 1, :], bias_rest))
            own.then(dve.tensor_tensor(bias_rest, bias_rest, bias_part[:, 1, :], ALU.subtract))
            dve.tensor_copy(bias_part[:, 2, :], bias_rest).then_inc(bias_parts_ready, 1)

            dve.wait_ge(lam_exp_ready, 1)
            own.then(dve.tensor_tensor(lam[:, 4:5], lam[:, 3:4], lam[:, 2:3], ALU.subtract))
            own.then(dve.tensor_scalar(lam[:, 5:6], lam[:, 4:5], LAMBDA_INIT, None, ALU.subtract))

            w = [dt_work[:, i, :] for i in range(8)]
            byh = lambda i: byhead[:, i, :].unsqueeze(1).broadcast_to([P, TT, SH])
            dve.wait_ge(dt_projected, 1)
            dve.tensor_copy(dtT, bank(6)[0:SH]).then_inc(dtt_copied, 1)
            dve.wait_ge(dt_projected, 2)
            own.then(dve.tensor_tensor(w[0].rearrange("p (t h) -> p t h", t=TT),
                                       bank(7, TT * SH).rearrange("p (t h) -> p t h", t=TT), byh(0), ALU.add))
            dve.scalar_tensor_tensor(out=w[1], in0=w[0], scalar=-1.0, in1=w[0], op0=ALU.mult, op1=ALU.min
                                     ).then_inc(dt_exp_asked, 1)
            own.mark(dve.tensor_scalar(w[3], w[0], 0.0, None, ALU.max))
            dve.wait_ge(dt_exp_ready, 1)
            own.then(dve.tensor_scalar(w[4], w[2], 2.0, None, ALU.add))
            own.then(dve.reciprocal(w[5], w[4]))
            own.then(dve.tensor_tensor(w[5], w[5], w[2], ALU.mult))
            own.then(dve.tensor_tensor(w[6], w[5], w[5], ALU.mult))
            own.then(dve.tensor_scalar(w[7], w[6], ATANH[0], None, ALU.mult))
            for a in ATANH[1:]:
                own.then(dve.scalar_tensor_tensor(out=w[7], in0=w[7], scalar=a, in1=w[6], op0=ALU.add, op1=ALU.mult))
            own.then(dve.scalar_tensor_tensor(out=w[7], in0=w[7], scalar=1.0, in1=w[5], op0=ALU.add, op1=ALU.mult))
            own.then(dve.scalar_tensor_tensor(out=dt[:].rearrange("p t h -> p (t h)"), in0=w[7], scalar=2.0, in1=w[3],
                                              op0=ALU.mult, op1=ALU.add))
            dve.scalar_tensor_tensor(out=dta[:], in0=dt[:], scalar=-1.0, in1=byh(1), op0=ALU.mult, op1=ALU.mult
                                     ).then_inc(dta_ready, 1)

            def take_output(h):
                dve.wait_ge(pv_done, h + 1)
                own.then(dve.tensor_copy(o_all[:, :, ds(h, 1), :].rearrange("p q a d -> p q (a d)"),
                                         bank(7).rearrange("p (q d) -> p q d", q=TT)))

            def attention(h0, reg=0):
                h = reg * 2 + h0
                split(attention_unit(2, h0, reg))
                dve.wait_ge(unit_used, attention_unit(1, h0, reg).number + 1)
                dve.tensor_copy(kT, bank(1)).then_inc(k_copied, 1)
                split(attention_unit(3, h0, reg))
                split(attention_unit(4, h0, reg))
                if h0 > 0:
                    take_output(h - 1)
                for q in range(TT):
                    w = P * (q + 1)
                    sc = probs[:, score_at[q]:score_at[q] + 2 * w]
                    dve.wait_ge(scores_done, h * TT + q + 1)
                    for m in range(2):
                        ins = dve.scalar_tensor_tensor(
                            out=sc[:, m * w:m * w + w], in0=negdist[:, SEQ - w:SEQ],
                            scalar=slopes[:, ds(h, 1)], in1=bank(3 + 2 * (q % 2) + m, w),
                            op0=ALU.mult, op1=ALU.add)
                    ins.then_inc(scores_drained, 1)
                    dve.wait_ge(scores_drained, h * TT + q + 1)
                    dve.tensor_reduce(amax[:, 2 * q:2 * q + 2], sc.rearrange("p (m w) -> p m w", m=2), AX,
                                      ALU.max, negate=True).then_inc(max_ready, 1)
                for q in range(TT):
                    w = P * (q + 1)
                    sc = probs[:, score_at[q]:score_at[q] + 2 * w]
                    dve.wait_ge(probs_ready, h * TT + q + 1)
                    own.then(dve.reciprocal(arec[:, 2 * q:2 * q + 2], asum[:, 2 * q:2 * q + 2]))
                    own.mark(dve.tensor_scalar(sc[:, 0:w], sc[:, 0:w], arec[:, 2 * q:2 * q + 1], None, ALU.mult))
                    own.then(dve.tensor_scalar(arec[:, 2 * q + 1:2 * q + 2], arec[:, 2 * q + 1:2 * q + 2],
                                               lam[:, 5:6], None, ALU.mult))
                    ins = dve.scalar_tensor_tensor(out=sc[:, 0:w], in0=sc[:, w:2 * w],
                                                   scalar=arec[:, 2 * q + 1:2 * q + 2], in1=sc[:, 0:w],
                                                   op0=ALU.mult, op1=ALU.add)
                    if q == TT - 1:
                        ins.then_inc(attn_ready, 1)

            attention(0)
            with dve.Fori(0, HEADS // 2 - 1) as i:
                own.round(i, 0, 2 * (1 + 3 * TT))
                attention(1, i)
                attention(2, i)
            own.rounds(HEADS // 2 - 1)
            attention(HEADS - 1)
            take_output(HEADS - 1)

            o3 = o_all.rearrange("p q h d -> p (q h) d")
            o_square = at(YST_AT, TT * HEADS, DV)
            own.then(dve.tensor_tensor(o_square, o3, o3, ALU.mult))
            dve.tensor_reduce(ostat[:, 0, :], o_square, AX, ALU.add).then_inc(o_squared, 1)

            def finish_attention():
                dve.wait_ge(o_rooted, 1)
                oroot = ostat[:, 1, :]
                own.then(dve.reciprocal(oroot, oroot))
                dve.tensor_tensor(o3, o3, oroot.unsqueeze(2).broadcast_to([P, TT * HEADS, DV]), ALU.mult
                                  ).then_inc(o_ready, 1)

            def conv_params(g):
                own.mark(dve.tensor_copy(gconv[:, :, 0:GT], conv_col[:, :, ds(GT * g, GT)]))
                own.mark(dve.tensor_copy(gconv[:, :, GT:GT + 1], conv_col[:, :, ds(GROUPS * GT + g, 1)]))
                own.mark(dve.tensor_copy(gconv[:, :, GT + 1:GT + 2], conv_col[:, :, ds(GROUPS * (GT + 1) + g, 1)]))
                own.mark(dve.tensor_copy(gconvb[:, 0:GT], par_convb[:, ds(GT * g, GT)]))
                own.mark(dve.tensor_copy(gconvb[:, GT:GT + 1], par_convb[:, ds(GROUPS * GT + g, 1)]))
                own.then(dve.tensor_copy(gconvb[:, GT + 1:GT + 2], par_convb[:, ds(GROUPS * (GT + 1) + g, 1)]))

            def convolve(g, n):
                split(Unit(SSD_UNITS + n + 2, g, 10))
                kind, i = SSD_ORDER[n]
                if kind == "z":
                    return
                i = {"x": i, "b": GT, "c": GT + 1}[kind]
                r, o = raw[:, CONV_AT[n] % 2, :], pre[:, i, :]
                if n == 0:
                    wait(dve, chunk_turned, TURNS * g)
                dve.wait_ge(proj_copied, 10 * g + n + 1)
                own.then(dve.tensor_scalar(o, r[:, TAPS - 1:RAW], gconv[:, TAPS - 1, i:i + 1], gconvb[:, i:i + 1],
                                           ALU.mult, ALU.add))
                for k in (2, 1, 0):
                    ins = dve.scalar_tensor_tensor(out=o, in0=r[:, k:k + SEQ], scalar=gconv[:, k, i:i + 1], in1=o,
                                                   op0=ALU.mult, op1=ALU.add)
                    if k:
                        own.then(ins)
                    else:
                        ins.then_inc(conv_done, 1)

            def scan_params(g):
                h = ds(HG * g, HG)
                wait(dve, ys_ready, TT * g)
                own.mark(dve.tensor_copy(gdt[:], dt[:, :, h]))
                own.mark(dve.tensor_copy(gdecay[:].rearrange("p c k h -> p (c k) h"),
                                         decay[:].rearrange("p c k h -> p (c k) h")[:, :, h]))
                own.mark(dve.tensor_copy(gskip[:], byhead[:, 2, h]))
                own.mark(dve.tensor_copy(gnorm[:], par_ssd[:, ds(GT * g, GT)]))
                dve.tensor_copy(gdta[:], dta[:, :, h]).then_inc(scan_params_ready, 1)
                dve.wait_ge(scan_params_ready, g + 1)

            def heads(v):
                return v.rearrange("p (r d) -> p r d", r=HG)

            def over_head(v):
                return v.unsqueeze(2).broadcast_to([P, HG, HD])

            def scan_first(g, c):
                if c == 0:
                    dve.wait_ge(chunk_copied, TURNS * (g + 1))
                wait(dve, state_summed, (TT - 1) * g + c)
                wait(dve, y_diag_done, TT * g + c)
                own.then(dve.tensor_tensor(heads(xdt), heads(x_tok[:, c, :]), over_head(gdt[:, c, :]), ALU.mult))
                dve.tensor_tensor(heads(xdte), heads(xdt), over_head(gdecay[:, c, 0, :]), ALU.mult
                                  ).then_inc(xdte_ready, 1)
                own.mark(dve.tensor_tensor(heads(y_tmp), heads(x_tok[:, c, :]), over_head(gskip[:]), ALU.mult))
                dve.wait_ge(cb_done, TT * g + c + 1)
                dve.tensor_tensor(cb[:], bank(2, P), upto[:], ALU.mult).then_inc(cb_read, 1)
                dve.wait_ge(cb_read, TT * g + c + 1)

            def scan_mix(g, c):
                dve.wait_ge(seg_ready, TT * g + c + 1)
                dve.tensor_tensor(seg, seg, cb[:].unsqueeze(1).broadcast_to([P, HG, P]), ALU.mult
                                  ).then_inc(mix_ready, 1)

            def scan_last(g, c):
                y = y_tok[:, c, :]
                if c:
                    dve.wait_ge(y_off_done, (TT - 1) * g + c)
                    own.then(dve.tensor_tensor(heads(y), heads(bank(6)), over_head(gdecay[:, c, 1, :]), ALU.mult))
                    own.then(dve.tensor_tensor(y, y, y_tmp, ALU.add))
                else:
                    own.then(dve.tensor_copy(y, y_tmp))
                dve.wait_ge(y_diag_done, TT * g + c + 1)
                dve.tensor_tensor(y, y, bank(5), ALU.add).then_inc(y_drained, 1)
                dve.wait_ge(y_drained, TT * g + c + 1)
                dve.tensor_tensor(y, y, z_act[:, c, :], ALU.mult).then_inc(y_gated, 1)
                if c < TT - 1:
                    dve.wait_ge(state_summed, (TT - 1) * g + c + 1)
                    if c:
                        own.then(dve.tensor_tensor(heads(state), heads(state), over_head(gdecay[:, c, 2, :]), ALU.mult))
                        dve.tensor_tensor(state, state, bank(2), ALU.add).then_inc(state_ready, 1)
                    else:
                        dve.tensor_copy(state, bank(2)).then_inc(state_ready, 1)
                    dve.wait_ge(state_ready, (TT - 1) * g + c + 1)

            def norm_group(g):
                dve.wait_ge(y_rooted, g + 1)
                own.then(dve.reciprocal(small[:, 8:12], small[:, 4:8]))
                dve.tensor_tensor(y_tok, y_tok, small[:, 8:12].unsqueeze(2).broadcast_to([P, TT, GW]), ALU.mult
                                  ).then_inc(y_normed, 1)

            def take_group(g):
                for c in range(TT):
                    dve.wait_ge(y_turned, TT * g + c + 1)
                    dve.tensor_tensor(ysT[:, ds(GT * g, GT), c * P:(c + 1) * P],
                                      bank(3 + c).rearrange("p (j t) -> p j t", j=GT),
                                      gnorm[:].unsqueeze(2).broadcast_to([P, GT, P]), ALU.mult).then_inc(ys_ready, 1)

            for b in range(2):
                own.mark(dve.memset(raw[:, b, 0:TAPS - 1], 0.0))
            conv_params(0)
            for n in range(10):
                convolve(0, n)
                if n == 0:
                    finish_attention()
            dve.wait_ge(decay_ready, 1)
            scan_params(0)
            with dve.Fori(1, GROUPS) as g:
                own.round(g, 1, 6 + 6 * 3 + 2 * TT + 1 + 2 * (TT - 1) + (TT - 2) + 1 + 4)
                conv_params(g)
                for c in range(TT):
                    scan_first(g - 1, c)
                    for n in QUARTER[c][:1]:
                        convolve(g, n)
                    scan_mix(g - 1, c)
                    for n in QUARTER[c][1:]:
                        convolve(g, n)
                    scan_last(g - 1, c)
                norm_group(g - 1)
                take_group(g - 1)
                scan_params(g)
            own.rounds(GROUPS - 1)
            for c in range(TT):
                scan_first(GROUPS - 1, c)
                scan_mix(GROUPS - 1, c)
                scan_last(GROUPS - 1, c)
            norm_group(GROUPS - 1)
            take_group(GROUPS - 1)

            for q in range(TT):
                dve.wait_ge(o_turned, q + 1)
                dve.tensor_scalar(yaT[:, :, q * P:(q + 1) * P],
                                  psum[:, (4 + 2 * (q % 2)) * 512 - 1024:(6 + 2 * (q % 2)) * 512 - 1024].rearrange(
                                      "p (h t) -> p h t", t=P), par_head, None, ALU.mult).then_inc(ya_ready, 1)

            def merge(d, last=False):
                dve.wait_ge(mg_projected, 2 * d + 1)
                dve.wait_ge(gates_ready, 2 * d + 1)
                own.mark(dve.tensor_tensor(part_a, gate_a, bank(2), ALU.mult))
                if not last:
                    split(Unit(GATE_UNITS + 2, d))
                    split(Unit(GATE_UNITS + 3, d))
                dve.wait_ge(mg_projected, 2 * d + 2)
                dve.wait_ge(gates_ready, 2 * d + 2)
                own.then(dve.tensor_tensor(gate_s, gate_s, bank(3), ALU.mult))
                dve.tensor_tensor(mergedT[:, ds(d, 1), :].rearrange("p a t -> p (a t)"), part_a, gate_s, ALU.add
                                  ).then_inc(mg_read, 1)

            merge(0)
            with dve.Fori(1, KT - 1) as d:
                own.round(d, 1, 2)
                merge(d)
            own.rounds(KT - 2)
            merge(KT - 1, last=True)

            dve.memset(arena[:, kb(MOE_AT + 28):kb(MOE_AT + 34)], 0.0).then_inc(bias_cleared, 1)

            def choose(t):
                dve.wait_ge(routed, t + 1)
                dve.tensor_tensor(logits[:, t, :], bank(6, EXPERTS), byhead[:, 3, :], ALU.add
                                  ).then_inc(logits_read, 1)
                dve.wait_ge(logits_read, t + 1)
                own.then(dve.max(top8[:, t, :], logits[:, t, :]))
                own.then(dve.max_index(top8_at[:, t, :], top8[:, t, :], logits[:, t, :]))
                idx = top_idx[:, t * TOPK:(t + 1) * TOPK]
                own.then(dve.tensor_copy(idx, top8_at[:, t, 0:TOPK]))
                oh = onehot[:, t * TOPK:(t + 1) * TOPK, :]
                own.then(dve.tensor_tensor(oh, iota_e[:].unsqueeze(1).broadcast_to([P, TOPK, EXPERTS]),
                                           idx.unsqueeze(2).broadcast_to([P, TOPK, EXPERTS]), ALU.is_equal))
                dve.tensor_reduce(chosen[:, t, :], oh.rearrange("p k e -> p e k"), AX, ALU.add
                                  ).then_inc(chosen_ready, 1)
                dve.tensor_scalar(top_exp[:, t, :], top8[:, t, 0:TOPK], top8[:, t, 0:1], None, ALU.subtract
                                  ).then_inc(top_asked, 1)

            def add_out(t):
                dve.wait_ge(out_projected, t + 1)
                dve.tensor_tensor(xs[:, t, :], xs[:, t, :], psum[:, (t % 2) * 1024:(t % 2) * 1024 + 1024], ALU.add
                                  ).then_inc(x1_ready, 1)

            add_out(0)
            for t in range(TT):
                if t + 1 < TT:
                    add_out(t + 1)
                normalize(1, t, xn)
                evacuate(1, t, par_moe, h_tile_of(t))
                if t:
                    choose(t - 1)
            choose(TT - 1)

            dve.wait_ge(ranked, 1)
            cnt, ov, tmp, inc, delta, one = (count[:, i, :] for i in range(6))
            own.mark(dve.tensor_copy(row_of.rearrange("p t e -> p (t e)"), bank(7, TT * EXPERTS)))
            own.then(dve.tensor_copy(cnt, bank(7, EXPERTS, TT * EXPERTS)))
            own.mark(dve.memset(one, 1.0))
            own.then(dve.tensor_scalar(ov, cnt, float(P), None, ALU.is_gt))
            for b in range(2, SEQ // P):
                own.then(dve.tensor_scalar(tmp, cnt, float(b * P), None, ALU.is_gt))
                own.then(dve.tensor_tensor(ov, ov, tmp, ALU.add))
            own.then(dve.tensor_tensor_scan(inc, one, ov, 0.0, ALU.mult, ALU.add))
            own.then(dve.tensor_tensor(delta, inc, ov, ALU.subtract))
            own.then(dve.scalar_tensor_tensor(out=delta, in0=delta, scalar=float(P), in1=iota_far[:],
                                              op0=ALU.mult, op1=ALU.add))
            own.then(dve.scalar_tensor_tensor(out=far, in0=row_of, scalar=float(P),
                                              in1=delta.unsqueeze(1).broadcast_to([P, TT, EXPERTS]),
                                              op0=ALU.is_ge, op1=ALU.mult))
            own.then(dve.tensor_tensor(row_of, row_of, far, ALU.add))
            own.then(dve.tensor_tensor(row_of, row_of, iota_row[:].unsqueeze(1).broadcast_to([P, TT, EXPERTS]), ALU.add))
            for t in range(TT):
                own.mark(dve.tensor_tensor(picked[:, t * TOPK:(t + 1) * TOPK, :], onehot[:, t * TOPK:(t + 1) * TOPK, :],
                                           row_of[:, t, :].unsqueeze(1).broadcast_to([P, TOPK, EXPERTS]), ALU.mult))
            own.wait()
            own.then(dve.tensor_reduce(row_f, picked, AX, ALU.add))
            own.mark(dve.tensor_copy(rows_u[:], row_f))
            own.mark(dve.tensor_copy(slot_info[:, :, 0].rearrange("p (t k) -> p t k", t=TT),
                                     token_id[:].unsqueeze(2).broadcast_to([P, TT, TOPK])))
            dve.wait_ge(top_exp_ready, 1)
            own.then(dve.tensor_reduce(top_sum[:, 0:TT], top_exp, AX, ALU.add))
            own.then(dve.reciprocal(top_sum[:, 4:4 + TT], top_sum[:, 0:TT]))
            dve.tensor_tensor(slot_info[:, :, 1].rearrange("p (t k) -> p t k", t=TT), top_exp,
                              top_sum[:, 4:4 + TT].unsqueeze(2).broadcast_to([P, TT, TOPK]), ALU.mult
                              ).then_inc(slots_ready, 1)
            own.then(dve.tensor_tensor(ended[0:1], inc[0:1, :].unsqueeze(1).broadcast_to([1, EXTRA, EXPERTS]),
                                       extra_id[:].unsqueeze(2).broadcast_to([1, EXTRA, EXPERTS]), ALU.is_le))
            own.then(dve.tensor_reduce(owner[0:1, 0:EXTRA], ended[0:1], AX, ALU.add))
            own.then(dve.tensor_scalar(owner[0:1, 0:EXTRA], owner[0:1, 0:EXTRA], float(EXPERTS - 1), None, ALU.min))
            own.mark(dve.tensor_copy(control[:, 0:EXTRA], owner[0:1, 0:EXTRA]))
            own.mark(dve.tensor_copy(control[:, EXTRA:EXTRA + 1], inc[0:1, EXPERTS - 1:EXPERTS]))

            dve.wait_ge(slots_turned, 1)
            dve.wait_ge(slots_stored, 16 * TT * TOPK)
            own.mark(dve.tensor_copy(slot_token[:], bank(6, BLOCKS)))
            own.wait()
            dve.tensor_copy(gate_tab[:], bank(6, BLOCKS, P)).then_inc(tables_ready, 1)

            def take_x(i):
                dve.wait_ge(x_turned, i + 1)
                dve.tensor_tensor(xgT, psum[:, 6 * 512:8 * 512].rearrange("p (k t) -> p k t", t=P),
                                  par_moe.unsqueeze(2).broadcast_to([P, KT, P]), ALU.mult).then_inc(xt_ready, 1)

            def take_act(i):
                dve.wait_ge(act_hi_ready, i + 1)
                dve.tensor_tensor(act_lo, psum[:, 6 * 512:8 * 512].rearrange("p (k t) -> p k t", t=P),
                                  act_hi.bitcast(F32), ALU.subtract).then_inc(actt_ready, 1)

            def split_x(i):
                dve.wait_ge(x_hi_ready, i + 1)
                dve.tensor_tensor(x_lo, xgT, x_hi.bitcast(F32), ALU.subtract).then_inc(x_lo_ready, 1)

            def split_piece(number, slot, rows):
                dve.wait_ge(hi_ready, number + 1)
                dve.tensor_tensor(piece_lo[slot], rows, piece_hi[slot].bitcast(F32), ALU.subtract
                                  ).then_inc(lo_ready, 1)

            def split_up(i, start):
                for k in range(start, start + 4):
                    split_piece(up_piece(i, k), k % 4, up_rows[k])

            def split_down(i, start):
                for k in range(start, start + 4):
                    split_piece(down_piece(i, k), k % 4, down_rows[k])

            def activate(i, half, mine):
                dve.wait_ge(up_done, 2 * i + half + 1)
                dve.tensor_scalar(g_sb, bank(2 * half), LIMIT, None, ALU.min).then_inc(g_ready, 1)
                mine.mark(dve.tensor_scalar(u_sb, bank(2 * half + 1), LIMIT, -LIMIT, ALU.min, ALU.max))
                mine.wait()
                mine.then(dve.scalar_tensor_tensor(out=t_sb, in0=u_sb, scalar=1.0, in1=g_sb, op0=ALU.add, op1=ALU.mult))
                dve.wait_ge(sig_ready, 2 * i + half + 1)
                wait(dve, act_turned, i)
                dve.tensor_tensor(hidden[:, half * HALF:(half + 1) * HALF], t_sb, sig_sb, ALU.mult
                                  ).then_inc(act_ready, 1)

            mine = Own(dve, hidden_own)

            def experts(first, end):
                take_x(first)
                split_x(first)
                split_up(first, 0)
                activate(first, 0, mine)
                split_up(first, 4)
                activate(first, 1, mine)
                take_x(first + 1)

                def round_of(b):
                    split_x(b)
                    split_up(b, 0)
                    activate(b, 0, mine)
                    split_up(b, 4)
                    take_act(b - 1)
                    split_down(b - 1, 0)
                    activate(b, 1, mine)
                    split_down(b - 1, 4)

                with dve.Fori(first + 1, end - 1) as b:
                    mine.round(b, first + 1, 4)
                    round_of(b)
                    take_x(b + 1)
                mine.rounds(end - first - 2)
                round_of(end - 1)
                take_act(end - 1)
                split_down(end - 1, 0)
                split_down(end - 1, 4)

            experts(0, EXPERTS)
            extra = dve.value_load(control[0:1, EXTRA:EXTRA + 1], min_val=0, max_val=EXTRA)
            with dve.If(extra > 0):
                experts(EXPERTS, BLOCKS)

            for n in range(TT * TOPK):
                t = n // TOPK
                dve.wait_ge(y_got_landed[n % 4], 16 * (n // 4 + 1))
                ins = dve.tensor_tensor(xs[:, t, :], xs[:, t, :], y_got[:, n % 4, :], ALU.add)
                ins.then_inc(y_got_added, 1)
                dve.wait_ge(y_got_added, n + 1)
                if n % TOPK == TOPK - 1:
                    normalize(2, t, xn_ple)
                    if t:
                        evacuate(2, t - 1, par_ple, h3T[:, :, (t - 1) * P:t * P])
            evacuate(2, TT - 1, par_ple, h3T[:, :, (TT - 1) * P:])

            for t in range(TT):
                dve.wait_ge(ple_sig_ready, t + 1)
                dve.wait_ge(ple_projected, PLE_DONE[t])
                o = (2 + 4 * (t % 2)) * 512
                own.then(dve.tensor_tensor(ple_gate, ple_gate, psum[:, o:o + 1024], ALU.mult))
                dve.tensor_tensor(xs[:, t, :], xs[:, t, :], ple_gate, ALU.add).then_inc(ple_added, 1)
                dve.wait_ge(end_rooted, t + 1)
                n = 3 * TT + t
                own.then(dve.reciprocal(stat[:, n, 0:1], stat[:, n, 1:2]))
                if t >= 2:
                    dve.wait_ge(out_stored[t % 2], 16 * (t // 2))
                dve.scalar_tensor_tensor(out=out_tile[:, t % 2, :], in0=xs[:, t, :], scalar=stat[:, n, 0:1],
                                         in1=final_w, op0=ALU.mult, op1=ALU.mult).then_inc(out_ready, 1)

        @block.tensor
        def _(pe):
            def mm(o, l, r, start, stop):
                return pe.matmul(o, l, r, start=start, stop=stop)

            def turn(t, n, buf, b):
                pe.wait_ge(xn_ready, n + 1)
                wait(pe, h_ready, n)
                for k in range(KT):
                    ins = pe.transpose(psum[:, b * 512 + k * P:b * 512 + k * P + P],
                                       buf[:, t % 2, k * P:(k + 1) * P], ident[:])
                ins.then_inc(xn_turned, 1)

            def mm3(o, l_hi, l_lo, r_hi, r_lo, start, stop):
                mm(o, l_hi, r_hi, start, False)
                mm(o, l_hi, r_lo, False, False)
                return mm(o, l_lo, r_hi, False, stop)

            def project_unit(out_ap, unit):
                pe.wait_ge(lo_ready, unit.number + 1)
                for k in range(KT):
                    ins = mm3(out_ap, w_hi[:, unit.slot, k], w_lo[:, unit.slot, k], h_hi[:, k], h_lo[:, k],
                              k == 0, k == KT - 1)
                ins.then_inc(unit_used, 1)

            def project(out_ap, w, rhs, kt=KT):
                for k in range(kt):
                    ins = mm(out_ap, w[:, k, :], rhs[:, k, :], k == 0, k == kt - 1)
                return ins

            pe.wait_ge(consts_ready, 1)
            pe.wait_ge(params_landed, 16 * PARAM_DMAS)
            pe.transpose(bank(7, NORMS), rows_a[0:NORMS, :], ident[0:NORMS, 0:NORMS])
            pe.transpose(bank(7, TAPS * CONV_TILES, P), rows_b[0:TAPS * CONV_TILES, :],
                         ident[0:TAPS * CONV_TILES, 0:TAPS * CONV_TILES]).then_inc(params_turned, 1)
            for t in range(TT):
                turn(t, t, xn, 4)

            pe.wait_ge(h_lo_ready, TT)
            pe.wait_ge(wdt_split, 2)
            for k in range(KT):
                ins = mm3(bank(6)[0:SH], wdt_hi[:, k], wdt_lo[:, k], h_hi[:, k], h_lo[:, k], k == 0, k == KT - 1)
            ins.then_inc(dt_projected, 1)
            pe.wait_ge(dtt_copied, 1)
            for t in range(TT):
                ins = pe.transpose(bank(7, SH, t * SH), dtT[:, t * P:(t + 1) * P], ident[0:SH, 0:SH])
            ins.then_inc(dt_projected, 1)

            at_col = {3: 0, 2: 512, 0: 896, 1: 1024}

            def attention(h0, reg=0, first=False, last=False):
                h = reg * 2 + h0
                if not last:
                    project_unit(bank(0), attention_unit(0, h0, reg))
                    project_unit(bank(1), attention_unit(1, h0, reg))
                if not first:
                    pe.wait_ge(attn_ready, h)
                    for q in range(TT):
                        for j in range(q + 1):
                            c = 3 * 512 + at_col[q] + j * P
                            ins = pe.transpose(psum[:, c:c + P], probs[:, score_at[q] + j * P:score_at[q] + (j + 1) * P],
                                               ident[:])
                    ins.then_inc(attn_turned, 1)
                if not last:
                    wait(pe, v_copied, h)
                    if first:
                        pe.wait_ge(dtt_copied, 1)
                    project_unit(bank(6), attention_unit(2, h0, reg))
                if not first:
                    pe.wait_ge(at_copied, h)
                    pe.wait_ge(v_copied, h)
                    for q in range(TT):
                        for j in range(q + 1):
                            ins = mm(bank(7, DV, q * DV), atT[:, at_col[q] + j * P:at_col[q] + (j + 1) * P],
                                     v_sb[:, j, :], j == 0, j == q)
                    ins.then_inc(pv_done, 1)
                if not last:
                    if first:
                        pe.wait_ge(dt_exp_asked, 1)
                    pe.wait_ge(vt_copied, h + 1)
                    for t in range(TT):
                        ins = pe.transpose(bank(2, DV, t * DV), vT[:, t * P:(t + 1) * P], ident[:])
                    ins.then_inc(v_turned, 1)
                    pe.wait_ge(q_copied, h + 1)
                    pe.wait_ge(k_copied, h + 1)
                    for q in range(TT):
                        if q >= 2:
                            pe.wait_ge(scores_drained, h * TT + q - 1)
                        for m in range(2):
                            rows = slice(m * DK, (m + 1) * DK)
                            ins = mm(bank(3 + 2 * (q % 2) + m, P * (q + 1)), qT[rows, q * P:(q + 1) * P],
                                     kT[rows, 0:P * (q + 1)], True, True)
                        ins.then_inc(scores_done, 1)

            attention(0, first=True)
            with pe.Fori(0, HEADS // 2 - 1) as i:
                attention(1, i)
                attention(2, i)
            attention(HEADS - 1)
            attention(HEADS, last=True)

            pe.wait_ge(dta_ready, 1)
            for c in range(TT):
                for kind, mask in enumerate((after, upto, ones)):
                    ins = mm(bank(5, SH, (3 * c + kind) * SH), mask[:], dta[:, c, :], True, True)
            ins.then_inc(decay_summed, 1)

            def project_tile(g, n):
                wait(pe, proj_copied, 10 * g + n - 1)
                project_unit(bank(n % 2), Unit(SSD_UNITS + n, g, 10))

            def turn_chunks(g):
                pe.wait_ge(silu_done, 7 * g + GT)
                wait(pe, y_gated, TT * g)
                for c in range(TT):
                    for j in range(GT):
                        ins = pe.transpose(bank(3 + c, P, j * P), pre[:, j, c * P:(c + 1) * P], ident[:])
                    ins.then_inc(chunk_turned, 1)
                pe.wait_ge(silu_done, 7 * g + GT + 1)
                for c in range(TT):
                    ins = pe.transpose(bank(7, P, c * P), BT[:, c * P:(c + 1) * P], ident[:])
                ins.then_inc(chunk_turned, 1)
                pe.wait_ge(silu_done, 7 * g + GT + 3)
                for c in range(TT):
                    pe.wait_ge(chunk_copied, TURNS * g + c + 1)
                    for j in range(GT):
                        ins = pe.transpose(bank(3 + c, P, j * P), pre[:, GT + 2 + j, c * P:(c + 1) * P], ident[:])
                    ins.then_inc(chunk_turned, 1)

            def scan_sums(g, c):
                if c == 0:
                    wait(pe, ys_ready, TT * g)
                    pe.wait_ge(silu_done, 7 * g + GT + 2)
                    pe.wait_ge(chunk_copied, TURNS * (g + 1))
                else:
                    pe.wait_ge(state_ready, (TT - 1) * g + c)
                cs = slice(c * P, (c + 1) * P)
                mm(bank(2, P), BT[:, cs], CT[:, cs], True, True).then_inc(cb_done, 1)
                pe.wait_ge(dta_after_ready, TT * g + c + 1)
                wait(pe, seg_ready, TT * g + c)
                for r in range(HG):
                    ins = mm(psum[:, 3 * 512 + r * P:3 * 512 + (r + 1) * P], dta_after[:, r, :], upto[:], True, True)
                ins.then_inc(seg_summed, 1)

            def scan_products(g, c):
                if c:
                    mm(bank(6), CT[:, c * P:(c + 1) * P], state, True, True).then_inc(y_off_done, 1)
                pe.wait_ge(mix_ready, TT * g + c + 1)
                pe.wait_ge(xdte_ready, TT * g + c + 1)
                wait(pe, y_drained, TT * g + c)
                for r in range(HG):
                    ins = mm(bank(5, HD, r * HD), seg[:, r, :], xdt[:, r * HD:(r + 1) * HD], True, True)
                ins.then_inc(y_diag_done, 1)
                if c < TT - 1:
                    pe.wait_ge(cb_read, TT * g + c + 1)
                    mm(bank(2), b_tok[:, c, :], xdte, True, True).then_inc(state_summed, 1)

            def turn_group(g):
                pe.wait_ge(y_normed, g + 1)
                for c in range(TT):
                    for j in range(GT):
                        ins = pe.transpose(bank(3 + c, P, j * P), y_tok[:, c, j * P:(j + 1) * P], ident[:])
                    ins.then_inc(y_turned, 1)

            for n in range(10):
                project_tile(0, n)
            pe.wait_ge(decay_ready, 1)
            pe.wait_ge(o_squared, 1)
            turn_chunks(0)
            with pe.Fori(1, GROUPS) as g:
                for c in range(TT):
                    for n in QUARTER[c][:1]:
                        project_tile(g, n)
                    scan_sums(g - 1, c)
                    for n in QUARTER[c][1:]:
                        project_tile(g, n)
                    scan_products(g - 1, c)
                turn_chunks(g)
                pe.wait_ge(chunk_copied, TURNS * (g + 1))
                turn_group(g - 1)
            pe.wait_ge(proj_copied, 10 * GROUPS)
            for c in range(TT):
                scan_sums(GROUPS - 1, c)
                if c < 2:
                    project_unit(bank(c), Unit(GATE_UNITS + c))
                scan_products(GROUPS - 1, c)

            pe.wait_ge(o_ready, 1)
            pe.wait_ge(y_drained, TT * GROUPS)
            turn_group(GROUPS - 1)
            for q in range(TT):
                pe.wait_ge(ys_ready, TT * GROUPS)
                wait(pe, ya_ready, q - 1)
                for h in range(HEADS):
                    c = (2 + 2 * (q % 2)) * 512 + h * P
                    ins = pe.transpose(psum[:, c:c + P], o_all[:, q, h, :], ident[:])
                ins.then_inc(o_turned, 1)

            def merge(d):
                if not isinstance(d, int):
                    pe.wait_ge(mg_read, d)
                else:
                    pe.wait_ge(ya_ready, TT)
                pe.wait_ge(w_mg_landed[0], 16 * (d + 1))
                project(bank(2), w_ya, yaT).then_inc(mg_projected, 1)
                if not isinstance(d, int):
                    for j in range(2):
                        project_unit(bank(j), Unit(GATE_UNITS + j, d))
                pe.wait_ge(w_mg_landed[1], 16 * (d + 1))
                project(bank(3), w_ys, ysT, SSD_IN // P).then_inc(mg_projected, 1)

            merge(0)
            with pe.Fori(1, KT) as d:
                merge(d)

            pe.wait_ge(w_o_landed, 32)
            pe.wait_ge(mg_read, KT)

            def out_proj(t):
                wait(pe, x1_ready, t - 1)
                for half in range(2):
                    for k in range(KT):
                        ins = mm(bank(2 * (t % 2) + half), mergedT[:, k, t * P:(t + 1) * P],
                                 w_o[:, k, half * 512:half * 512 + 512], k == 0, k == KT - 1)
                ins.then_inc(out_projected, 1)

            def route(t):
                pe.wait_ge(h_ready, TT + t + 1)
                pe.wait_ge(w_r_landed, 16)
                wait(pe, logits_read, t)
                for k in range(KT):
                    ins = mm(bank(6, EXPERTS), h_tile_of(t)[:, k], w_r[:, k, :], k == 0, k == KT - 1)
                ins.then_inc(routed, 1)

            def rank(t):
                pe.wait_ge(chosen_ready, t + 1)
                for u in range(t + 1):
                    mm(bank(7, EXPERTS, t * EXPERTS), (before if u == t else ones)[:], chosen[:, u, :],
                       u == 0, u == t)

            out_proj(0)
            out_proj(1)
            for t in range(TT):
                turn(t, TT + t, xn, 4)
                if t + 2 < TT:
                    out_proj(t + 2)
                route(t)
            for t in range(TT):
                rank(t)
            for u in range(TT):
                ins = mm(bank(7, EXPERTS, TT * EXPERTS), ones[:], chosen[:, u, :], u == 0, u == TT - 1)
            ins.then_inc(ranked, 1)

            pe.wait_ge(slot_rows_landed, 16)
            pe.wait_ge(logits_read, TT)
            pe.transpose(bank(6, BLOCKS), slot_rows[0:BLOCKS, :, 0], ident[0:BLOCKS, 0:BLOCKS])
            pe.transpose(bank(6, BLOCKS, P), slot_rows[0:BLOCKS, :, 1], ident[0:BLOCKS, 0:BLOCKS]
                         ).then_inc(slots_turned, 1)

            def turn_x(i):
                pe.wait_ge(xg_landed, 16 * (i + 1))
                wait(pe, actt_ready, i - 1)
                for k in range(KT):
                    ins = pe.transpose(psum[:, 6 * 512 + k * P:6 * 512 + (k + 1) * P], xg[:, k * P:(k + 1) * P], ident[:])
                ins.then_inc(x_turned, 1)

            def turn_act(i):
                pe.wait_ge(act_ready, 2 * i + 2)
                for k in range(KT):
                    ins = pe.transpose(psum[:, 6 * 512 + k * P:6 * 512 + (k + 1) * P], hidden[:, k * P:(k + 1) * P], ident[:])
                ins.then_inc(act_turned, 1)

            def piece(number, k, l_hi, l_lo, b):
                pe.wait_ge(lo_ready, number + 1)
                for n in range(2):
                    ins = mm3(bank(b + n), l_hi[:, k, :], l_lo[:, k, :], piece_hi[k % 4][:, n, :],
                              piece_lo[k % 4][:, n, :], k == 0, False)
                ins.then_inc(unit_used, 1)

            def up(i, half):
                pe.wait_ge(xt_ready, i + 1)
                wait(pe, act_ready, 2 * (i - 1) + half + 1)
                if half == 0:
                    for c in range(UNITS):
                        pe.wait_ge(w_up_landed[0][c], 32 * (i + 1))
                        for j in range(2):
                            for u in range(2):
                                ins = mm(bank(u), xgT[:, 2 * c + j, :], w_unit_up[0][c][:, j, u, :],
                                         c == 0 and j == 0, False)
                        ins.then_inc(up_used, 1)
                else:
                    pe.wait_ge(x_lo_ready, i + 1)
                    for k in range(KT):
                        piece(up_piece(i, k), k, x_hi, x_lo, 2)
                pe.wait_ge(bias_up_landed, 16 * (i + 1))
                for u in range(2):
                    o = u * FF + half * HALF
                    ins = mm(bank(2 * half + u), ones_bf[:], bias_up[:, o:o + HALF], False, True)
                ins.then_inc(up_done, 1)

            def down(i):
                pe.wait_ge(actt_ready, i + 1)
                wait(pe, y_ready, i)
                for k in range(KT):
                    piece(down_piece(i, k), k, act_hi, act_lo, 4)
                pe.wait_ge(bias_dn_landed, 16 * (i + 1))
                for n in range(2):
                    ins = mm(bank(4 + n), ones_bf[:], bias_dn[:, n * 512:(n + 1) * 512], False, True)
                ins.then_inc(down_done, 1)

            def round_of(b):
                up(b, 0)
                turn_act(b - 1)
                up(b, 1)
                turn_x(b + 1)
                down(b - 1)

            def experts(first, end):
                turn_x(first)
                up(first, 0)
                up(first, 1)
                turn_x(first + 1)
                round_of(first + 1)
                with pe.Fori(first + 2, end - 1) as b:
                    round_of(b)
                up(end - 1, 0)
                turn_act(end - 2)
                up(end - 1, 1)
                down(end - 2)
                turn_act(end - 1)
                down(end - 1)

            pe.wait_ge(tables_ready, 1)
            experts(0, EXPERTS)
            extra = pe.value_load(control[0:1, EXTRA:EXTRA + 1], min_val=0, max_val=EXTRA)
            with pe.If(extra > 0):
                experts(EXPERTS, BLOCKS)

            pe.wait_ge(ple_in_landed, 48)
            for k in range(2):
                for t in range(TT):
                    c = 6 * 512 + (k * TT + t) * P
                    ins = pe.transpose(psum[:, c:c + P], p_sb[:, t, k * P:(k + 1) * P], ident[:])
            ins.then_inc(p_turned, 1)

            def embed(t):
                wait(pe, ple_added, t - 1)
                for half in range(2):
                    for k in range(2):
                        ins = mm(bank(2 + 4 * (t % 2) + half), pT[:, k, t * P:(t + 1) * P],
                                 w_pp[:, k, half * 512:half * 512 + 512], k == 0, k == 1)
                ins.then_inc(ple_projected, 1)

            def gate(t):
                pe.wait_ge(h_ready, 2 * TT + t + 1)
                wait(pe, ple_sig_ready, t)
                for half in range(2):
                    for k in range(KT):
                        ins = mm(bank(half), h3T[:, k, t * P:(t + 1) * P], w_pg[:, k, half * 512:half * 512 + 512],
                                 k == 0, k == KT - 1)
                ins.then_inc(ple_projected, 1)

            pe.wait_ge(p_ready, 1)
            embed(0)
            embed(1)
            pe.wait_ge(y_ready, EXPERTS)
            for t in range(TT):
                turn(t, 2 * TT + t, xn_ple, 4)
            pe.wait_ge(w_pg_landed, 16)
            gate(0)
            gate(1)
            for t in range(2, TT):
                embed(t)
                gate(t)


_INS = ["x", "p", "mix_norm_w", "w_in", "lambda_q1", "lambda_k1", "lambda_q2", "lambda_k2", "da_head_norm_w",
        "w_attn_branch", "conv_w", "conv_b", "dt_bias", "a_log", "d_skip", "ssd_norm_w", "w_ssd_branch", "w_out",
        "moe_norm_w", "router_w", "router_b", "w_up", "b_up", "w_down", "b_down", "ple_norm_w", "w_ple_gate",
        "w_ple_proj", "final_norm_w"]


def kernel(**inputs):
    import numpy as np
    import concourse.bacc as bacc
    from concourse.bass_utils import run_bass_kernel_spmd

    nc = bacc.Bacc("TRN2", target_bir_lowering=False, num_devices=1)
    arrays, args = {}, []
    for name in _INS:
        a = np.ascontiguousarray(inputs[name])
        arrays[f"in_{name}"] = a
        args.append(nc.dram_tensor(f"in_{name}", a.shape, mybir.dt.from_np(a.dtype), kind="ExternalInput").ap())
    out = nc.dram_tensor("out_y", (1, SEQ, D), F32, kind="ExternalOutput").ap()
    build(nc, *args, out)
    r = run_bass_kernel_spmd(nc, [arrays], core_ids=[0])
    return r.results[0]["out_y"]
```
